# Optimizing a Trainium2 kernel written in Bass

```python
import math
import jax, jax.numpy as jnp
from jax import lax
import numpy as np

D_MODEL = 1024
BATCH = 1
SEQ = 256
DEPTH = 2
DEC_BATCH = 8
DEC_SEQ = 8
PAST_LEN = 2048
PAGE_SIZE = 128

D_MIX = D_MODEL
D_SSD = D_MIX // 2
SSD_HEAD_DIM = 64
N_SSD_HEADS = D_SSD // SSD_HEAD_DIM
N_SSD_GROUPS = 2
SSD_HEADS_PER_GROUP = N_SSD_HEADS // N_SSD_GROUPS
D_STATE = 128
CONV_W = 4
CONV_DIM = D_SSD + 2 * N_SSD_GROUPS * D_STATE
D_ATTN = D_MIX - D_SSD
HEAD_DIM = 64
N_Q_HEADS = D_ATTN // HEAD_DIM
N_KV_HEADS = 2
Q_PER_KV = N_Q_HEADS // N_KV_HEADS
KV_DIM = N_KV_HEADS * HEAD_DIM
WINDOW = 128
BLOCK = 128
ROPE_THETA = 10000.0
N_META = 16
META_PAD = (-N_META) % BLOCK
IN_DIM = D_SSD + CONV_DIM + N_SSD_HEADS + D_ATTN + 2 * KV_DIM
D_FF = 2816
N_EXPERTS = 8
TOP_K = 2
MOE_BLOCK = 128
N_DENSE = (DEPTH + 1) // 2
N_MOE = DEPTH // 2
EPS = 1e-6
NEG = -1e30
ATTN_SCALE = HEAD_DIM ** -0.5

kernel_name = 'hymba_ssd_swa_sink_moe_step'

def rmsnorm(x, w):
    xf = x.astype(jnp.float32)
    y = xf * lax.rsqrt(jnp.mean(xf * xf, axis=-1, keepdims=True) + EPS)
    return (y * w.astype(jnp.float32)).astype(x.dtype)

def rope(x, pos):
    half = HEAD_DIM // 2
    inv_freq = ROPE_THETA ** (-jnp.arange(half, dtype=jnp.float32) / half)
    ang = pos.astype(jnp.float32)[:, None] * inv_freq[None, :]
    cos = jnp.cos(ang)[:, None, :]
    sin = jnp.sin(ang)[:, None, :]
    xf = x.astype(jnp.float32)
    x1, x2 = xf[..., :half], xf[..., half:]
    return jnp.concatenate([x1 * cos - x2 * sin, x2 * cos + x1 * sin], -1).astype(x.dtype)

def split_in(p):
    idx = np.cumsum([D_SSD, CONV_DIM, N_SSD_HEADS, D_ATTN, KV_DIM]).tolist()
    return jnp.split(p, idx, axis=-1)

def causal_conv(u, prev, w, b):
    up = jnp.concatenate([prev, u], axis=1)
    t = u.shape[1]
    out = b + sum(up[:, k:k + t] * w[k] for k in range(CONV_W))
    return jax.nn.silu(out), up[:, up.shape[1] - (CONV_W - 1):]

def ssd_scan(x, dt, a, bm, cm, h0, chunk):
    bsz, L = x.shape[:2]
    nc = L // chunk
    G, R, P, N = N_SSD_GROUPS, SSD_HEADS_PER_GROUP, SSD_HEAD_DIM, D_STATE
    f32 = jnp.float32
    xf = x.astype(f32).reshape(bsz, nc, chunk, G, R, P)
    dtc = dt.reshape(bsz, nc, chunk, G, R)
    bc = bm.astype(f32).reshape(bsz, nc, chunk, G, N)
    cc = cm.astype(f32).reshape(bsz, nc, chunk, G, N)
    cs = jnp.cumsum(dtc * a.reshape(G, R), axis=2)
    xdt = xf * dtc[..., None]
    seg = cs[:, :, :, None] - cs[:, :, None, :]
    tril = jnp.tril(jnp.ones((chunk, chunk), bool))[:, :, None, None]
    decay = jnp.where(tril, jnp.exp(jnp.where(tril, seg, 0.0)), 0.0)
    cb = jnp.einsum('bcign,bcjgn->bcijg', cc, bc)
    y_diag = jnp.einsum('bcijgr,bcjgrp->bcigrp', decay * cb[..., None], xdt)
    last = cs[:, :, -1:]
    states = jnp.einsum('bcjgn,bcjgr,bcjgrp->bcgrpn', bc, jnp.exp(last - cs), xdt)
    chunk_dec = jnp.exp(last[:, :, 0])

    def step(h, inp):
        st, dc = inp
        return h * dc[..., None, None] + st, h

    h_fin, h_prev = lax.scan(step, h0.astype(f32).reshape(bsz, G, R, P, N),
                             (jnp.moveaxis(states, 1, 0), jnp.moveaxis(chunk_dec, 1, 0)))
    h_prev = jnp.moveaxis(h_prev, 0, 1)
    y_off = jnp.einsum('bcign,bcgrpn,bcigr->bcigrp', cc, h_prev, jnp.exp(cs))
    y = (y_diag + y_off).reshape(bsz, L, N_SSD_HEADS, P)
    return y, h_fin.reshape(bsz, N_SSD_HEADS, P, N)

def ssd_branch(z, xbc, dt_raw, conv_prev, h0, valid, chunk, lp):
    bsz, L = z.shape[:2]
    xbc_c, conv_new = causal_conv(xbc, conv_prev, lp['conv_w'], lp['conv_b'])
    xs, bm, cm = jnp.split(xbc_c, [D_SSD, D_SSD + N_SSD_GROUPS * D_STATE], axis=-1)
    xs = xs.reshape(bsz, L, N_SSD_HEADS, SSD_HEAD_DIM)
    bm = bm.reshape(bsz, L, N_SSD_GROUPS, D_STATE)
    cm = cm.reshape(bsz, L, N_SSD_GROUPS, D_STATE)
    dt = jax.nn.softplus(dt_raw.astype(jnp.float32) + lp['dt_bias'].astype(jnp.float32))
    if valid is not None:
        dt = dt * valid[None, :, None]
    a = -jnp.exp(lp['a_log'].astype(jnp.float32))
    y, h_new = ssd_scan(xs, dt, a, bm, cm, h0, chunk)
    y = y + lp['d_skip'].astype(jnp.float32)[:, None] * xs.astype(jnp.float32)
    y = y.reshape(bsz, L, D_SSD) * jax.nn.silu(z.astype(jnp.float32))
    gs = D_SSD // N_SSD_GROUPS
    y = rmsnorm(y.reshape(bsz, L, N_SSD_GROUPS, gs), lp['ssd_norm_w'].reshape(N_SSD_GROUPS, gs))
    return y.reshape(bsz, L, D_SSD).astype(z.dtype), h_new, conv_new

def attn_prep(q, k, v, pos, lp):
    bsz, t = q.shape[:2]
    q = rope(rmsnorm(q.reshape(bsz, t, N_Q_HEADS, HEAD_DIM), lp['q_norm_w']), pos)
    k = rope(rmsnorm(k.reshape(bsz, t, N_KV_HEADS, HEAD_DIM), lp['k_norm_w']), pos)
    return q, k, v.reshape(bsz, t, N_KV_HEADS, HEAD_DIM)

def visible(pos_q, pos_band):
    pos_meta = jnp.arange(N_META, dtype=jnp.int32)
    pq = pos_q[..., :, None]
    meta = pos_meta <= pq
    pk = pos_band[..., None, :]
    band = (pk >= N_META) & (pk <= pq) & (pq - pk < WINDOW)
    return jnp.concatenate([meta, band], axis=-1)

def sink_probs(s, sinks):
    sk = sinks.astype(jnp.float32).reshape(N_KV_HEADS, Q_PER_KV)[:, :, None, None]
    m = jnp.maximum(jnp.max(s, axis=-1, keepdims=True), sk)
    e = jnp.exp(s - m)
    return e / (jnp.sum(e, axis=-1, keepdims=True) + jnp.exp(sk - m))

def swa_prompt(q, k, v, pos, sinks):
    bsz, Lp = q.shape[:2]
    nb = Lp // BLOCK
    qb = q.reshape(bsz, nb, BLOCK, N_KV_HEADS, Q_PER_KV, HEAD_DIM)
    kb = k.reshape(bsz, nb, BLOCK, N_KV_HEADS, HEAD_DIM)
    vb = v.reshape(bsz, nb, BLOCK, N_KV_HEADS, HEAD_DIM)
    shift = lambda t: jnp.pad(t[:, :-1], ((0, 0), (1, 0), (0, 0), (0, 0), (0, 0)))
    k_band = jnp.concatenate([shift(kb), kb], axis=2)
    v_band = jnp.concatenate([shift(vb), vb], axis=2)
    pos_b = pos.reshape(nb, BLOCK)
    pos_band = jnp.concatenate([jnp.pad(pos_b[:-1], ((1, 0), (0, 0)), constant_values=-1), pos_b], axis=1)
    k_meta = k[:, META_PAD:META_PAD + N_META]
    v_meta = v[:, META_PAD:META_PAD + N_META]
    mask = visible(pos_b, pos_band)
    s_meta = jnp.einsum('bnqkgd,bjkd->bnkgqj', qb, k_meta, preferred_element_type=jnp.float32)
    s_band = jnp.einsum('bnqkgd,bnjkd->bnkgqj', qb, k_band, preferred_element_type=jnp.float32)
    s = jnp.concatenate([s_meta, s_band], axis=-1) * ATTN_SCALE
    s = jnp.where(mask[None, :, None, None], s, NEG)
    p = sink_probs(s, sinks).astype(v.dtype)
    o = (jnp.einsum('bnkgqj,bjkd->bnqkgd', p[..., :N_META], v_meta)
         + jnp.einsum('bnkgqj,bnjkd->bnqkgd', p[..., N_META:], v_band))
    return o.reshape(bsz, Lp, D_ATTN)

def swa_sample(q, k, v, k_meta, v_meta, k_win, v_win, sinks):
    bsz, t = q.shape[:2]
    pos_q = PAST_LEN + jnp.arange(t, dtype=jnp.int32)
    pos_band = jnp.concatenate([PAST_LEN - WINDOW + jnp.arange(WINDOW, dtype=jnp.int32), pos_q])
    k_band = jnp.concatenate([k_win.astype(k.dtype), k], axis=1)
    v_band = jnp.concatenate([v_win.astype(v.dtype), v], axis=1)
    mask = visible(pos_q, pos_band)
    qg = q.reshape(bsz, t, N_KV_HEADS, Q_PER_KV, HEAD_DIM)
    km = k_meta.astype(k.dtype)
    vm = v_meta.astype(v.dtype)
    s_meta = jnp.einsum('bqkgd,bjkd->bkgqj', qg, km, preferred_element_type=jnp.float32)
    s_band = jnp.einsum('bqkgd,bjkd->bkgqj', qg, k_band, preferred_element_type=jnp.float32)
    s = jnp.where(mask, jnp.concatenate([s_meta, s_band], axis=-1) * ATTN_SCALE, NEG)
    p = sink_probs(s, sinks).astype(v.dtype)
    o = (jnp.einsum('bkgqj,bjkd->bqkgd', p[..., :N_META], vm)
         + jnp.einsum('bkgqj,bjkd->bqkgd', p[..., N_META:], v_band))
    nw = k_band.shape[1] - WINDOW
    return o.reshape(bsz, t, D_ATTN), k_band[:, nw:], v_band[:, nw:]

def merge_out(y_ssd, y_att, lp):
    return jnp.concatenate([y_ssd, rmsnorm(y_att, lp['attn_norm_w'])], axis=-1) @ lp['w_out']

def mixer_prompt(h, lp):
    bsz, L = h.shape[:2]
    Lp = L + META_PAD
    proj = jnp.pad(h @ lp['w_in'], ((0, 0), (META_PAD, 0), (0, 0)))
    pos = jnp.arange(Lp, dtype=jnp.int32) - META_PAD
    valid = (pos >= 0).astype(jnp.float32)
    z, xbc, dt_raw, q, k, v = split_in(proj)
    conv0 = jnp.zeros((bsz, CONV_W - 1, CONV_DIM), proj.dtype)
    h0 = jnp.zeros((bsz, N_SSD_HEADS, SSD_HEAD_DIM, D_STATE), jnp.float32)
    y_ssd, ssm_new, conv_new = ssd_branch(z, xbc, dt_raw, conv0, h0, valid, BLOCK, lp)
    q, k, v = attn_prep(q, k, v, pos, lp)
    y_att = swa_prompt(q, k, v, pos, lp['sinks'])
    y = merge_out(y_ssd[:, META_PAD:], y_att[:, META_PAD:], lp)
    return y, ssm_new, conv_new, k[:, META_PAD:META_PAD + N_META], v[:, META_PAD:META_PAD + N_META], k[:, Lp - WINDOW:], v[:, Lp - WINDOW:]

def mixer_sample(h, st_ssm, st_conv, c_meta_k, c_meta_v, c_win_k, c_win_v, lp):
    bsz, t = h.shape[:2]
    proj = h @ lp['w_in']
    pos = PAST_LEN + jnp.arange(t, dtype=jnp.int32)
    z, xbc, dt_raw, q, k, v = split_in(proj)
    y_ssd, ssm_new, conv_new = ssd_branch(z, xbc, dt_raw, st_conv.astype(proj.dtype), st_ssm, None, t, lp)
    q, k, v = attn_prep(q, k, v, pos, lp)
    y_att, k_win_new, v_win_new = swa_sample(q, k, v, c_meta_k, c_meta_v, c_win_k, c_win_v, lp['sinks'])
    return merge_out(y_ssd, y_att, lp), ssm_new, conv_new, k_win_new, v_win_new

def swiglu(h, wg, wu, wd):
    return (jax.nn.silu(h @ wg) * (h @ wu)) @ wd

def moe_ffn(h, w_router, wg, wu, wd):
    shp = h.shape
    hf = h.reshape(-1, D_MODEL)
    n = hf.shape[0]
    nr = n * TOP_K
    logits = (hf @ w_router).astype(jnp.float32)
    top_v, top_i = lax.top_k(logits, TOP_K)
    gates = jax.nn.softmax(top_v, axis=-1)
    flat_e = top_i.reshape(-1)
    flat_t = jnp.repeat(jnp.arange(n, dtype=jnp.int32), TOP_K)
    flat_g = gates.reshape(-1)
    order = jnp.argsort(flat_e)
    se = flat_e[order]
    counts = jnp.bincount(flat_e, length=N_EXPERTS)
    starts = jnp.cumsum(counts) - counts
    padded = (counts + MOE_BLOCK - 1) // MOE_BLOCK * MOE_BLOCK
    pad_end = jnp.cumsum(padded)
    pad_start = pad_end - padded
    dest = pad_start[se] + (jnp.arange(nr, dtype=jnp.int32) - starts[se])
    n_blocks = -(-(nr + N_EXPERTS * (MOE_BLOCK - 1)) // MOE_BLOCK)
    m = n_blocks * MOE_BLOCK
    row_tok = jnp.full((m,), n, jnp.int32).at[dest].set(flat_t[order])
    row_gate = jnp.zeros((m,), jnp.float32).at[dest].set(flat_g[order])
    blk_e = jnp.minimum(jnp.searchsorted(pad_end, jnp.arange(n_blocks) * MOE_BLOCK, side='right'), N_EXPERTS - 1)
    h_ext = jnp.concatenate([hf, jnp.zeros((1, D_MODEL), hf.dtype)], axis=0)
    xb = h_ext[row_tok].reshape(n_blocks, MOE_BLOCK, D_MODEL)

    def one_block(args):
        xe, e = args
        return swiglu(xe, wg[e], wu[e], wd[e])

    yb = lax.map(one_block, (xb, blk_e)).reshape(m, D_MODEL)
    out = jax.ops.segment_sum(yb * row_gate[:, None].astype(yb.dtype), row_tok, num_segments=n + 1)[:n]
    return out.reshape(shp)

def setup_inputs(seed: int = 0) -> dict:
    key = jax.random.key(seed)
    ks = iter(jax.random.split(key, 48))
    f32 = jnp.float32

    def nrm(shape, scale):
        return jax.random.normal(next(ks), shape, f32) * scale

    def gain(shape):
        return 1.0 + nrm(shape, 0.02)

    dt0 = jnp.exp(jax.random.uniform(next(ks), (DEPTH, N_SSD_HEADS), f32, math.log(1e-3), math.log(1e-1)))
    return {
        'x_prompt': nrm((BATCH, SEQ, D_MODEL), 1.0),
        'x_sample': nrm((DEC_BATCH, DEC_SEQ, D_MODEL), 1.0),
        'state_ssm': nrm((DEPTH, DEC_BATCH, N_SSD_HEADS, SSD_HEAD_DIM, D_STATE), 0.5),
        'state_conv': nrm((DEPTH, DEC_BATCH, CONV_W - 1, CONV_DIM), 1.0),
        'cache_meta_k': nrm((DEPTH, DEC_BATCH, N_META, N_KV_HEADS, HEAD_DIM), 1.0),
        'cache_meta_v': nrm((DEPTH, DEC_BATCH, N_META, N_KV_HEADS, HEAD_DIM), 1.0),
        'cache_win_k': nrm((DEPTH, DEC_BATCH, WINDOW, N_KV_HEADS, HEAD_DIM), 1.0),
        'cache_win_v': nrm((DEPTH, DEC_BATCH, WINDOW, N_KV_HEADS, HEAD_DIM), 1.0),
        'meta_tokens': nrm((N_META, D_MODEL), 1.0),
        'norm_mix_w': gain((DEPTH, D_MODEL)),
        'w_in': nrm((DEPTH, D_MODEL, IN_DIM), D_MODEL ** -0.5),
        'conv_w': nrm((DEPTH, CONV_W, CONV_DIM), CONV_W ** -0.5),
        'conv_b': nrm((DEPTH, CONV_DIM), 0.02),
        'dt_bias': dt0 + jnp.log(-jnp.expm1(-dt0)),
        'a_log': jnp.log(jax.random.uniform(next(ks), (DEPTH, N_SSD_HEADS), f32, 1.0, 16.0)),
        'd_skip': gain((DEPTH, N_SSD_HEADS)),
        'ssd_norm_w': gain((DEPTH, D_SSD)),
        'q_norm_w': gain((DEPTH, HEAD_DIM)),
        'k_norm_w': gain((DEPTH, HEAD_DIM)),
        'sinks': nrm((DEPTH, N_Q_HEADS), 0.5),
        'attn_norm_w': gain((DEPTH, D_ATTN)),
        'w_out': nrm((DEPTH, D_MIX, D_MODEL), D_MIX ** -0.5),
        'norm_ffn_w': gain((DEPTH, D_MODEL)),
        'w_gate': nrm((N_DENSE, D_MODEL, D_FF), D_MODEL ** -0.5),
        'w_up': nrm((N_DENSE, D_MODEL, D_FF), D_MODEL ** -0.5),
        'w_down': nrm((N_DENSE, D_FF, D_MODEL), D_FF ** -0.5),
        'w_router': nrm((N_MOE, D_MODEL, N_EXPERTS), D_MODEL ** -0.5),
        'moe_w_gate': nrm((N_MOE, N_EXPERTS, D_MODEL, D_FF), D_MODEL ** -0.5),
        'moe_w_up': nrm((N_MOE, N_EXPERTS, D_MODEL, D_FF), D_MODEL ** -0.5),
        'moe_w_down': nrm((N_MOE, N_EXPERTS, D_FF, D_MODEL), D_FF ** -0.5),
    }

def reference(x_prompt, x_sample, state_ssm, state_conv, cache_meta_k, cache_meta_v, cache_win_k, cache_win_v,
              meta_tokens, norm_mix_w, w_in, conv_w, conv_b, dt_bias, a_log, d_skip, ssd_norm_w,
              q_norm_w, k_norm_w, sinks, attn_norm_w, w_out, norm_ffn_w, w_gate, w_up, w_down,
              w_router, moe_w_gate, moe_w_up, moe_w_down):
    bsz = x_prompt.shape[0]
    meta = jnp.broadcast_to(meta_tokens.astype(x_prompt.dtype)[None], (bsz, N_META, D_MODEL))
    xp = jnp.concatenate([meta, x_prompt], axis=1)
    xs = x_sample
    p_ssm, p_conv, p_mk, p_mv, p_wk, p_wv = [], [], [], [], [], []
    s_ssm, s_conv, s_wk, s_wv = [], [], [], []
    for l in range(DEPTH):
        lp = {'w_in': w_in[l], 'conv_w': conv_w[l], 'conv_b': conv_b[l], 'dt_bias': dt_bias[l],
              'a_log': a_log[l], 'd_skip': d_skip[l], 'ssd_norm_w': ssd_norm_w[l],
              'q_norm_w': q_norm_w[l], 'k_norm_w': k_norm_w[l], 'sinks': sinks[l],
              'attn_norm_w': attn_norm_w[l], 'w_out': w_out[l]}
        yp, ssm_p, conv_p, mk_p, mv_p, wk_p, wv_p = mixer_prompt(rmsnorm(xp, norm_mix_w[l]), lp)
        xp = xp + yp
        ys, ssm_s, conv_s, wk_s, wv_s = mixer_sample(rmsnorm(xs, norm_mix_w[l]), state_ssm[l], state_conv[l],
                                                      cache_meta_k[l], cache_meta_v[l],
                                                      cache_win_k[l], cache_win_v[l], lp)
        xs = xs + ys
        i = l // 2
        hp = rmsnorm(xp, norm_ffn_w[l])
        hs = rmsnorm(xs, norm_ffn_w[l])
        if l % 2 == 0:
            xp = xp + swiglu(hp, w_gate[i], w_up[i], w_down[i])
            xs = xs + swiglu(hs, w_gate[i], w_up[i], w_down[i])
        else:
            xp = xp + moe_ffn(hp, w_router[i], moe_w_gate[i], moe_w_up[i], moe_w_down[i])
            xs = xs + moe_ffn(hs, w_router[i], moe_w_gate[i], moe_w_up[i], moe_w_down[i])
        p_ssm.append(ssm_p); p_conv.append(conv_p); p_mk.append(mk_p); p_mv.append(mv_p)
        p_wk.append(wk_p); p_wv.append(wv_p)
        s_ssm.append(ssm_s); s_conv.append(conv_s); s_wk.append(wk_s); s_wv.append(wv_s)
    return (xp[:, N_META:], xs,
            jnp.stack(p_ssm), jnp.stack(p_conv), jnp.stack(p_mk), jnp.stack(p_mv),
            jnp.stack(p_wk), jnp.stack(p_wv),
            jnp.stack(s_ssm), jnp.stack(s_conv), jnp.stack(s_wk), jnp.stack(s_wv))


_drawn_inputs = setup_inputs


def setup_inputs(seed=0):
    import zlib

    import numpy as np

    out = dict(_drawn_inputs(seed))
    spreads = {}
    factors = {'d_skip': 29.701, 'q_norm_w': 3.477, 'k_norm_w': 2.707, 'sinks': 5.305}
    for name, (base, spread) in spreads.items():
        noise = np.random.default_rng([zlib.crc32(name.encode()), seed]).standard_normal(out[name].shape)
        drawn = base * np.exp(spread * noise) if base else spread * noise
        out[name] = __import__('jax').numpy.asarray(drawn.astype(out[name].dtype))
    for name, factor in factors.items():
        out[name] = (out[name] * factor).astype(out[name].dtype)
    return out
```

```python
from contextlib import ExitStack

import numpy as np

import concourse.bass as bass
from concourse import mybir

F32 = mybir.dt.float32
U32 = mybir.dt.uint32
I32 = mybir.dt.int32
ALU = mybir.AluOpType
ACT = mybir.ActivationFunctionType
AX = mybir.AxisListType

D = 1024
DK = D // 128
LAYERS = 2
META, SEQ = 16, 256
NP = META + SEQ
SB, ST = 8, 8
NT = NP + SB * ST
TILES = ((0, 128), (128, 128), (256, NT - 256))
HEADS, STATE, CONV_W = 8, 128, 4
NPAD = NP + 3 + SB * (ST + 3)
RAWC = NP + (SB + 1) * (ST + 3)
NCONV = NPAD - 3
S0 = NP + 3
WIN = 128
FF = 2816
FC = FF // 128
EXPERTS = 8
SLOTS = 128
PASSES = -(-NT // SLOTS)
EPS = 1e-6
NEG = -1e30
PAST = 2048
RING, SLAB = 11, 2048
GU_SLABS = FC
DOWN_SLABS = FC // 2
FFN_SLABS = GU_SLABS + DOWN_SLABS
IN_SLABS, OUT_SLABS = 9, 4

UPPER = ((0, NT), (128, NT), (256, NT))
UOFF = (0, NT, NT + NT - 128)
UCOLS = NT + (NT - 128) + (NT - 256)
LOWER = (128, 256, NT)
LOFF = (0, 128, 384)
LCOLS = 128 + 256 + NT

PARAM_ROWS = 64
R_MIX, R_FFN, R_CW, R_CB, R_SSD, R_ATT = 0, 8, 16, 48, 56, 60


def constants():
    t = np.arange(NT)
    seq = np.where(t < NP, 0, 1 + (t - NP) // ST)
    same = seq[:, None] == seq[None, :]
    upper = (same & (t[:, None] <= t[None, :])).astype(np.float32)
    lower = (same & (t[:, None] > t[None, :])).astype(np.float32)

    def rows(a):
        return np.pad(a, ((0, 128 - a.shape[0]), (0, 0)))

    parts = {"ident": np.eye(128, dtype=np.float32)}
    parts["upper"] = np.concatenate([rows(upper[a:a + n, UPPER[i][0]:]) for i, (a, n) in enumerate(TILES)], 1)
    parts["lower"] = np.concatenate([rows(lower[a:a + n, :LOWER[i]]) for i, (a, n) in enumerate(TILES)], 1)
    parts["halves"] = np.kron(np.eye(2), np.ones((64, 64))).astype(np.float32)
    turn = np.zeros((128, 128), np.float32)
    for m in range(128):
        if m % 64 < 32:
            turn[m + 32, m] = -1.0
        else:
            turn[m - 32, m] = 1.0
    parts["turn"] = turn
    pos = np.where(t < NP, t, PAST + (t - NP) % ST).astype(np.float32)
    inv = np.float32(10000.0) ** (-np.arange(32, dtype=np.float32) / np.float32(32))
    ang = (pos[None, :] * inv[np.arange(128) % 32][:, None]).astype(np.float32).astype(np.float64)
    parts["cos"] = np.cos(ang).astype(np.float32)
    parts["sin"] = np.sin(ang).astype(np.float32)

    def mask(ok):
        return rows(np.where(ok, 0.0, NEG).astype(np.float32))

    def prompt(i0, ni, nj):
        i, j = np.arange(i0, i0 + ni)[:, None], np.arange(nj)[None, :]
        return mask((j <= i) & ((j < META) | (i - j < WIN)))

    parts["mask0"] = prompt(0, 128, 128)
    parts["mask1"] = prompt(128, 128, 256)
    parts["mask2"] = prompt(256, NP - 256, NP)
    tq = (np.arange(128) % ST)[:, None]
    w, n = np.arange(WIN)[None, :], np.arange(ST)[None, :]
    parts["mask_s"] = mask(np.concatenate([w > tq, np.ones((128, META), bool), n <= tq], 1))
    parts["batch"] = rows(np.concatenate([np.zeros((NP - 256, SB)), np.kron(np.eye(SB), np.ones((ST, 1)))]).astype(np.float32))
    parts["iota"] = np.tile(np.arange(128, dtype=np.float32), (128, 1))
    at, n = {}, 0
    for name, a in parts.items():
        at[name] = (n, a.shape[1])
        n += a.shape[1]
    return np.ascontiguousarray(np.concatenate(list(parts.values()), 1), dtype=np.float32), at


CONST, CONST_AT = constants()


def bc(ap, axis, n):
    a = ap.unsqueeze(axis)
    shape = list(a.shape)
    shape[axis] = n
    return a.to_broadcast(shape)


def weight_loads(a, l):
    whole = slice(0, 128)

    def cols(w, c0, n=256):
        return [(whole, lambda s: s.rearrange("p (k n) -> p k n", k=DK), w[:, c0:c0 + n].rearrange("(k p) n -> p k n", p=128))]

    w = a["w_in"][l]
    slabs = [cols(w, 2056)]
    for half in range(2):
        loads = []
        for cc in range(2):
            for g in range(2):
                c0 = 1544 + g * 256 + (2 * half + cc) * 64
                loads.append((whole, lambda s, o=cc * 128 + g * 64: s.rearrange("p (k n) -> p k n", k=DK)[:, :, o:o + 64],
                              w[:, c0:c0 + 64].rearrange("(k p) n -> p k n", p=128)))
        slabs.append(loads)
    slabs += [cols(w, 512 + 256 * i) for i in range(4)]
    slabs += [cols(w, 256 * i) for i in range(2)]
    w = a["w_out"][l]
    for i in range(OUT_SLABS):
        c0 = 256 * i
        loads = [(whole, lambda s: s.rearrange("p (k n) -> p k n", k=DK)[:, 0:4, :],
                  w[0:512, c0:c0 + 256].rearrange("(k p) n -> p k n", p=128))]
        for g in range(2):
            loads.append((slice(64 * g, 64 * g + 64), lambda s: s.rearrange("p (k n) -> p k n", k=DK)[:, 4:8, :],
                          w[512 + 256 * g:768 + 256 * g, c0:c0 + 256].rearrange("(c d) n -> d c n", d=64)))
        slabs.append(loads)
    if l == 0:
        for u in range(FC // 2):
            slabs.append(cols(a["w_gate"][0], 256 * u))
            slabs.append(cols(a["w_up"][0], 256 * u))
        blocks = [(half, f) for half in range(2) for f in range(FC)]
        for i in range(DOWN_SLABS):
            loads = []
            for half in range(2):
                mine = [(j, f) for j, (h, f) in enumerate(blocks[4 * i:4 * i + 4]) if h == half]
                if mine:
                    j0, f0, n = mine[0][0], mine[0][1], len(mine)
                    loads.append((whole, lambda s, j0=j0, n=n: s.rearrange("p (j n) -> p j n", j=4)[:, j0:j0 + n, :],
                                  a["w_down"][0][f0 * 128:(f0 + n) * 128, 512 * half:512 * half + 512]
                                  .rearrange("(j p) n -> p j n", p=128)))
            slabs.append(loads)
    return slabs


def hymba_step(nc, a, o):
    fixed = weight_loads(a, 0) + weight_loads(a, 1)
    seen = [0] * RING
    arrives = []
    for n, loads in enumerate(fixed):
        seen[n % RING] += 16 * len(loads)
        arrives.append(seen[n % RING])
    fixed_seen = list(seen)
    FIRST = (0, IN_SLABS + OUT_SLABS + FFN_SLABS)
    MOE0 = len(fixed)
    scope = ExitStack()
    with scope:
        def sb(name, cols, dt=F32, rows=128):
            return scope.enter_context(nc.sbuf_tensor(name, [rows, cols], dt))

        def sem(name):
            return scope.enter_context(nc.semaphore(name))

        bank = [scope.enter_context(nc.psum_tensor(f"bank{i}", [128, 512], F32)) for i in range(8)]
        const = sb("const", CONST.shape[1])
        ring = sb("ring", RING * SLAB)
        xT_ = sb("xT", DK * NT)
        hnT_ = sb("hnT", DK * NT)
        params = sb("params", 128)
        small = sb("small", 512)
        arena_cols = 20900
        arena = sb("arena", arena_cols)
        index8 = sb("index8", 24, U32)
        crowded = sb("crowded", 1, I32)

        def C(name):
            at, n = CONST_AT[name]
            return const[:, at:at + n]

        ident, halves, turn, cosT, sinT, iota = (C(x) for x in ("ident", "halves", "turn", "cos", "sin", "iota"))
        upper, lower = C("upper"), C("lower")
        xT = xT_[:, :].rearrange("p (k t) -> p k t", k=DK)
        hnT = hnT_[:, :].rearrange("p (k t) -> p k t", k=DK)
        mixT = hnT
        slots = [ring[:, i * SLAB:(i + 1) * SLAB] for i in range(RING)]

        at = [0]

        def take(n):
            at[0] += n
            assert at[0] <= arena_cols, at[0]
            return arena[:, at[0] - n:at[0]]

        qk_ = take(5 * NT)
        qk = qk_.rearrange("p (k t) -> p k t", k=5)
        zs = take(4 * NT).rearrange("p (k t) -> p k t", k=4)
        raw_ = take(DK * RAWC)
        raw = raw_.rearrange("p (k t) -> p k t", k=DK)
        xbc = raw_[:, 0:DK * NT].rearrange("p (k t) -> p k t", k=DK)
        conv_ = take(DK * NPAD)
        conv = conv_.rearrange("p (k t) -> p k t", k=DK)
        attn = [conv_[:, i * 1088:(i + 1) * 1088] for i in range(2)]
        xdt = take(3 * 512).rearrange("p (i n) -> p i n", i=3)
        Btok = take(3 * 256).rearrange("p (i n) -> p i n", i=3)
        ktok = take(3 * 128).rearrange("p (i n) -> p i n", i=3)
        vtok = take(3 * 128).rearrange("p (i n) -> p i n", i=3)
        h0_ = take(1024)
        h0 = h0_.rearrange("p (b n) -> p b n", b=SB)
        h0T_ = take(1024)
        h0T = h0T_.rearrange("p (b n) -> p b n", b=SB)
        tmp2 = [arena[:, at[0] - 2048 + 1008 * i:at[0] - 2048 + 1008 * (i + 1)].rearrange("p (j t) -> p j t", j=3)
                for i in range(2)]
        Bexp_ = take(1024)
        Bexp = Bexp_.rearrange("p (b n) -> p b n", b=SB)
        tails = Bexp_
        decay = [take(UCOLS) for _ in range(2)]
        cbm = take(UCOLS)
        tail_cols = decay[0][:, 0:27 * DK].rearrange("p (k n) -> p k n", k=DK)
        qs = decay[1][:, 0:256].rearrange("p (b c t) -> p b c t", b=SB, c=4)
        xw = take(384).rearrange("p (i n) -> p i n", i=3)
        pst = take(128)
        yoff = take(64)
        eoff = take(64)
        winK = take(512).rearrange("p (b n) -> p b n", b=4)
        winV = take(512).rearrange("p (b n) -> p b n", b=4)
        mnV = take(512).rearrange("p (b n) -> p b n", b=4)
        winKT = cbm[:, 0:512]
        metK = take(128)
        metKT = cbm[:, 512:576]
        sprob_ = take(304)
        sprob = sprob_.rearrange("p (g n) -> p g n", g=2)
        sprobT = take(512)
        rstd = take(NT)
        rstd_m = take(NT)
        wdt = take(64).rearrange("p (k n) -> p k n", k=DK)
        xtok_in = arena[:, 9 * NT:9 * NT + 3 * D]
        xtok_in = xtok_in.rearrange("p (i n) -> p i n", i=3)
        hidT = arena[:, 0:FC * NT].rearrange("p (f t) -> p f t", f=FC)
        gate_s = [arena[:, FC * NT + i * NT:FC * NT + (i + 1) * NT] for i in range(2)]
        rstd_f = rstd_m
        hn_tok = arena[:, 0:3072].rearrange("p (i n) -> p i n", i=3)
        x_tok = arena[:, 3072:6144].rearrange("p (i n) -> p i n", i=3)
        hid = arena[:, 6144:6144 + FC * SLOTS].rearrange("p (f s) -> p f s", f=FC)
        xg_ = arena[:, 9000:10024]
        xg = xg_.rearrange("p (k s) -> p k s", k=DK)
        ytok = arena[:, 10100:11124]
        pick = arena[:, 11200:11584].rearrange("p (i s) -> p i s", i=3)
        gpick = arena[:, 11600:11984].rearrange("p (i s) -> p i s", i=3)
        gpickT = arena[:, 12000:12000 + NT]
        gsil = [arena[:, 12400 + 128 * i:12528 + 128 * i] for i in range(2)]
        route = arena[:, 12700:13100]
        wr = arena[:, 13200:13264].rearrange("p (k n) -> p k n", k=DK)

        def R(i, n=24, w=8):
            return route[:, i:i + n].rearrange("p (i e) -> p i e", e=w)

        sm = [0]

        def little(n):
            sm[0] += n
            assert sm[0] <= 512
            return small[:, sm[0] - n:sm[0]]

        eps = little(1)
        qkw = [little(1) for _ in range(4)]
        dskip = [little(4) for _ in range(LAYERS)]
        sinks = [little(8) for _ in range(LAYERS)]
        sink_s = [little(2) for _ in range(LAYERS)]
        dtb = [little(8) for _ in range(LAYERS)]
        alog = [little(8) for _ in range(LAYERS)]
        nega = little(8)
        dt = little(24).rearrange("p (i h) -> p i h", i=3)
        dta = little(24).rearrange("p (i h) -> p i h", i=3)
        dw = [little(24) for _ in range(5)]
        negcs = little(24).rearrange("p (i h) -> p i h", i=3)
        wdec = little(24).rearrange("p (i h) -> p i h", i=3)
        mx = [little(3) for _ in range(2)]
        nm = [little(3) for _ in range(2)]
        sums = [little(3) for _ in range(2)]
        es = [little(3) for _ in range(2)]
        csrow = rstd[0:8, :]
        ones = sb("ones", 128)

        slab_here = [sem(f"slab_here{i}") for i in range(RING)]
        slab_free = sem("slab_free")
        const_here, tokens_here, params_here, small_here = sem("const_here"), sem("tokens_here"), sem("params_here"), sem("small_here")
        dtw_here, conv_rows_here, caches_here, router_here = sem("dtw_here"), sem("conv_rows_here"), sem("caches_here"), sem("router_here")
        mnv_new_here, h0_here = sem("mnv_new_here"), sem("h0_here")
        states_stored, kv_stored, outputs_stored = sem("states_stored"), sem("kv_stored"), sem("outputs_stored")
        set_up, params_psum, params_ready = sem("set_up"), sem("params_psum"), sem("params_ready")
        xin_psum, xT_ready = sem("xin_psum"), sem("xT_ready")
        squares_ready, sum_psum, rstd_ready, hn_ready = sem("squares_ready"), sem("sum_psum"), sem("rstd_ready"), sem("hn_ready")
        prev_psum, prev_ready = sem("prev_psum"), sem("prev_ready")
        proj_psum, proj_dve, proj_raw, proj_z = sem("proj_psum"), sem("proj_dve"), sem("proj_raw"), sem("proj_z")
        qksq_ready, qksum_psum, qkrstd_ready, qkn_ready, rot_psum, qk_ready = (
            sem(x) for x in ("qksq_ready", "qksum_psum", "qkrstd_ready", "qkn_ready", "rot_psum", "qk_ready"))
        conv_ready, xbc_ready, tail_psum, tail_ready = sem("conv_ready"), sem("xbc_ready"), sem("tail_psum"), sem("tail_ready")
        dt_exp_in, dt_exp, dt_ln_in, dt_ln, dta_ready, cs_psum, cs_ready, wdec_ready = (
            sem(x) for x in ("dt_exp_in", "dt_exp", "dt_ln_in", "dt_ln", "dta_ready", "cs_psum", "cs_ready", "wdec_ready"))
        tok_psum, tok_ready = sem("tok_psum"), sem("tok_ready")
        tail_cols_ready, qs_ready = sem("tail_cols_ready"), sem("qs_ready")
        score_psum, negmax_ready, exp_ready, prob_ready, probT_psum, probT_ready, att_psum, att_ready = (
            sem(x) for x in ("score_psum", "negmax_ready", "exp_ready", "prob_ready", "probT_psum", "probT_ready", "att_psum", "att_ready"))
        s_KT_psum, s_KT_ready, s_score_psum, s_negmax_ready, s_exp_ready, s_prob_ready, s_probT_psum, s_probT_ready, s_att_psum, s_att_ready = (
            sem(x) for x in ("s_KT_psum", "s_KT_ready", "s_score_psum", "s_negmax_ready", "s_exp_ready", "s_prob_ready",
                             "s_probT_psum", "s_probT_ready", "s_att_psum", "s_att_ready"))
        cb_psum, cb_ready, seg_psum, seg_ready, decay_exp, M_ready, ydiag_psum, yoff_psum, eoff_ready, y_ready = (
            sem(x) for x in ("cb_psum", "cb_ready", "seg_psum", "seg_ready", "decay_exp", "M_ready", "ydiag_psum", "yoff_psum", "eoff_ready", "y_ready"))
        Bexp_ready, h0T_psum, h0T_ready, xw_ready, pstate_psum, pstate_ready, sstate_psum, sstate_ready = (
            sem(x) for x in ("Bexp_ready", "h0T_psum", "h0T_ready", "xw_ready", "pstate_psum", "pstate_ready", "sstate_psum", "sstate_ready"))
        mixsq_ready, mixsum_psum, mixrstd_ready, mix_ready, out_psum = (
            sem(x) for x in ("mixsq_ready", "mixsum_psum", "mixrstd_ready", "mix_ready", "out_psum"))
        gu_psum, silu_ready, hid_ready, down_psum = sem("gu_psum"), sem("silu_ready"), sem("hid_ready"), sem("down_psum")
        logit_psum, gates_in, gates_exp, picks_counted, count_psum, route_ready = (
            sem(x) for x in ("logit_psum", "gates_in", "gates_exp", "picks_counted", "count_psum", "route_ready"))
        turn_psum, turn_act = sem("turn_psum"), sem("turn_act")
        pick_ready, xg_psum, xg_ready, pickT_psum, pickT_ready = (sem(x) for x in ("pick_ready", "xg_psum", "xg_ready", "pickT_psum", "pickT_ready"))
        y_psum, ytok_ready, comb_psum, comb_added, all_added = (sem(x) for x in ("y_psum", "ytok_ready", "comb_psum", "comb_added", "all_added"))
        dve_step, act_step = sem("dve_step"), sem("act_step")

        block = scope.enter_context(nc.Block())
        first_pass = 0

        def slab(n):
            return slots[n % RING]

        def wait_slab(pe, n):
            pe.wait_ge(slab_here[n % RING], arrives[n])

        @block.sync
        def _(sp):
            for n, loads in enumerate(fixed):
                if n >= RING:
                    sp.wait_ge(slab_free, n - RING + 1)
                for rows, view, src in loads:
                    sp.dma_start(view(slab(n)[rows, :]), src).then_inc(slab_here[n % RING], 16)

            def expert_slabs(k, e):
                for j in range(FFN_SLABS):
                    s = (MOE0 + j) % RING
                    sp.wait_ge(slab_free, k * FFN_SLABS + (MOE0 + j - RING + 1))
                    if j < GU_SLABS:
                        w = a["moe_w_gate"] if j % 2 == 0 else a["moe_w_up"]
                        c0 = 256 * (j // 2)
                        dst = slots[s].rearrange("p (k n) -> p k n", k=DK)
                        src = w[0, e, :, c0:c0 + 256].rearrange("(k p) n -> p k n", p=128)
                    else:
                        r0 = 256 * (j - GU_SLABS)
                        dst = slots[s].rearrange("p (r n) -> p r n", r=2)
                        src = a["moe_w_down"][0, e, r0:r0 + 256, :].rearrange("(r p) n -> p r n", p=128)
                    sp.dma_start(dst, src).then_inc(slab_here[s], 16)

            with sp.Fori(0, EXPERTS) as e:
                expert_slabs(e, e)
            sp.wait_ge(route_ready, 1)
            fullest = sp.value_load(crowded[0:1, 0:1], min_val=0, max_val=NT)
            with sp.If(fullest > SLOTS):
                with sp.Fori(1, PASSES) as b:
                    with sp.Fori(0, EXPERTS) as e:
                        expert_slabs(b * EXPERTS + e, e)

        @block.gpsimd
        def _(pool):
            pool.memset(ones[:, :], 1.0).then_inc(set_up, 1)
            pool.memset(small[:, :], 0.0).then_inc(set_up, 1)
            pool.wait_ge(set_up, 2)
            pool.memset(eps, EPS).then_inc(set_up, 1)
            with nc.allow_non_contiguous_dma(reason="small tables"):
                pool.dma_start(const[:, :], a["const"]).then_inc(const_here, 16)
                xp, xs, mt = a["x_prompt"][0], a["x_sample"].rearrange("b t d -> (b t) d"), a["meta_tokens"]
                pool.dma_start(xtok_in[0:META, 0, :], mt).then_inc(tokens_here, 16)
                pool.dma_start(xtok_in[META:128, 0, :], xp[0:112, :]).then_inc(tokens_here, 16)
                pool.dma_start(xtok_in[:, 1, :], xp[112:240, :]).then_inc(tokens_here, 16)
                pool.dma_start(xtok_in[0:16, 2, :], xp[240:256, :]).then_inc(tokens_here, 16)
                pool.dma_start(xtok_in[16:80, 2, :], xs).then_inc(tokens_here, 16)
                prow = tails[:, 0:128]
                for l in range(LAYERS):
                    r = PARAM_ROWS * l

                    def row(r0, n, src):
                        pool.dma_start(prow[r + r0:r + r0 + n, :], src).then_inc(params_here, 16)

                    row(R_MIX, 8, a["norm_mix_w"][l].rearrange("(k p) -> k p", p=128))
                    row(R_FFN, 8, a["norm_ffn_w"][l].rearrange("(k p) -> k p", p=128))
                    row(R_CW, 32, a["conv_w"][l].rearrange("w (k p) -> (w k) p", p=128))
                    row(R_CB, 8, a["conv_b"][l].rearrange("(k p) -> k p", p=128))
                    row(R_SSD, 4, a["ssd_norm_w"][l].rearrange("(k p) -> k p", p=128))
                    for g in range(2):
                        pool.dma_start(prow[r + R_ATT:r + R_ATT + 4, 64 * g:64 * g + 64],
                                       a["attn_norm_w"][l][256 * g:256 * g + 256].rearrange("(c d) -> c d", d=64)).then_inc(params_here, 16)
                    pool.wait_ge(set_up, 3)
                    for g in range(2):
                        half = slice(64 * g, 64 * g + 64)
                        pool.dma_start(qkw[2 * l][half, :], a["k_norm_w"][l].rearrange("(d o) -> d o", o=1)).then_inc(small_here, 16)
                        pool.dma_start(qkw[2 * l + 1][half, :], a["q_norm_w"][l].rearrange("(d o) -> d o", o=1)).then_inc(small_here, 16)
                        pool.dma_start(dskip[l][half, :], a["d_skip"][l][g:8:2].partition_broadcast(64)).then_inc(small_here, 16)
                    pool.dma_start(sinks[l], a["sinks"][l].partition_broadcast(128)).then_inc(small_here, 16)
                    pool.dma_start(dtb[l], a["dt_bias"][l].partition_broadcast(128)).then_inc(small_here, 16)
                    pool.dma_start(alog[l], a["a_log"][l].partition_broadcast(128)).then_inc(small_here, 16)
                    for r in range(16):
                        pool.dma_start(sink_s[l][8 * r:8 * r + 8, :], a["sinks"][l][r % 4:8:4].partition_broadcast(8)).then_inc(small_here, 16)

                def sample_caches(l, half):
                    bs = slice(4 * half, 4 * half + 4)
                    pool.dma_start(winK, a["cache_win_k"][l, bs].rearrange("b w g d -> w b (g d)")).then_inc(caches_here, 16)
                    pool.dma_start(winV, a["cache_win_v"][l, bs].rearrange("b w g d -> w b (g d)")).then_inc(caches_here, 16)
                    pool.dma_start(metK[0:64, :], a["cache_meta_k"][l, bs].rearrange("b w g d -> (b w) (g d)")).then_inc(caches_here, 16)
                    pool.dma_start(mnV[0:META, :, :], a["cache_meta_v"][l, bs].rearrange("b w g d -> w b (g d)")).then_inc(caches_here, 16)

                def new_values(half):
                    for b in range(4):
                        r0 = 16 + 8 * (4 * half + b)
                        pool.dma_start(mnV[META:META + ST, b, :], vtok[r0:r0 + ST, 2, :]).then_inc(mnv_new_here, 16)

                for l in range(LAYERS):
                    if l:
                        pool.wait_ge(xT_ready, 24)
                    else:
                        pool.wait_ge(params_psum, 1)
                    pool.dma_start(wdt, a["w_in"][l][:, 1536:1544].rearrange("(k p) n -> p k n", p=128)).then_inc(dtw_here, 16)
                    pool.dma_start(tails[0:24, :], a["state_conv"][l].rearrange("b r n -> (b r) n")).then_inc(conv_rows_here, 16)
                    sample_caches(l, 0)
                    for kind, src, dst in (("k", a["cache_win_k"], o["s_win_k"]), ("v", a["cache_win_v"], o["s_win_v"])):
                        pool.dma_start(dst[l, :, 0:WIN - ST].rearrange("b w g d -> b w (g d)"),
                                       src[l, :, ST:WIN].rearrange("b w g d -> b w (g d)")).then_inc(outputs_stored, 16)
                    pool.wait_ge(tail_ready, 2 * (l + 1))
                    pool.dma_start(o["p_conv"][l, 0], tails[0:3, :]).then_inc(kv_stored, 16)
                    pool.dma_start(o["s_conv"][l].rearrange("b r n -> (b r) n"), tails[3:27, :]).then_inc(kv_stored, 16)
                    pool.wait_ge(tok_ready, 8 * (l + 1))
                    pool.wait_ge(proj_dve, 7 * l + 1)
                    new_values(0)
                    for name, t in (("k", ktok), ("v", vtok)):
                        def rows(ap):
                            return ap.rearrange("w g d -> w (g d)")
                        pool.dma_start(rows(o[f"p_meta_{name}"][l, 0]), t[0:META, 0, :]).then_inc(outputs_stored, 16)
                        pool.dma_start(rows(o[f"p_win_{name}"][l, 0, 0:112]), t[16:128, 1, :]).then_inc(outputs_stored, 16)
                        pool.dma_start(rows(o[f"p_win_{name}"][l, 0, 112:128]), t[0:16, 2, :]).then_inc(outputs_stored, 16)
                        for b in range(SB):
                            pool.dma_start(rows(o[f"s_win_{name}"][l, b, WIN - ST:WIN]), t[16 + 8 * b:24 + 8 * b, 2, :]).then_inc(outputs_stored, 16)
                    pool.wait_ge(s_att_psum, 2 * l + 1)
                    pool.wait_ge(mnv_new_here, 16 * (8 * l + 4))
                    sample_caches(l, 1)
                    new_values(1)
                    for pr in range(4):
                        n = 4 * l + pr
                        if pr == 0:
                            pool.wait_ge(qk_ready, 5 * (l + 1))
                        else:
                            pool.wait_ge(states_stored, 32 * n)
                        pool.dma_start(h0, a["state_ssm"][l, :, 2 * pr:2 * pr + 2].rearrange("b h p n -> (h p) b n")).then_inc(h0_here, 16)
                        pool.wait_ge(pstate_ready, n + 1)
                        pool.dma_start(o["p_ssm"][l, 0, 2 * pr:2 * pr + 2].rearrange("h p n -> (h p) n"), pst).then_inc(states_stored, 16)
                        pool.wait_ge(sstate_ready, 2 * (n + 1))
                        pool.dma_start(o["s_ssm"][l, :, 2 * pr:2 * pr + 2].rearrange("b h p n -> (h p) b n"), h0).then_inc(states_stored, 16)
                pool.wait_ge(xT_ready, 32)
                pool.dma_start(wr, a["w_router"][0].rearrange("(k p) n -> p k n", p=128)).then_inc(router_here, 16)
                pool.wait_ge(all_added, 1)
                yp, ys = o["y_prompt"][0], o["y_sample"].rearrange("b t d -> (b t) d")
                pool.dma_start(yp[0:112, :], x_tok[META:128, 0, :]).then_inc(outputs_stored, 16)
                pool.dma_start(yp[112:240, :], x_tok[:, 1, :]).then_inc(outputs_stored, 16)
                pool.dma_start(yp[240:256, :], x_tok[0:16, 2, :]).then_inc(outputs_stored, 16)
                pool.dma_start(ys, x_tok[16:80, 2, :]).then_inc(outputs_stored, 16)
            pool.wait_ge(outputs_stored, 16 * (LAYERS * (2 + 2 * (3 + SB)) + 4))
            pool.wait_ge(kv_stored, 32 * LAYERS)
            pool.wait_ge(states_stored, 32 * 4 * LAYERS)

        @block.tensor
        def _(pe):
            mm = nc.tensor.matmul
            owed = [0]

            def pay(ins):
                if owed[0]:
                    ins.then_inc(slab_free, 1)
                    owed[0] -= 1
                return ins

            def norm_sums(n):
                pe.wait_ge(squares_ready, n + 1)
                for k in range(DK):
                    i = mm(bank[0][:, 0:NT], ones[:, :], hnT[:, k, :], start=(k == 0), stop=(k == DK - 1))
                    if k < DK - 1:
                        pay(i)
                i.then_inc(sum_psum, 1)

            pe.wait_ge(const_here, 16)
            pe.wait_ge(set_up, 3)
            pe.wait_ge(params_here, 16 * 7 * LAYERS)
            nc.tensor.transpose(bank[7][:, 0:128], tails[:, 0:128], ident).then_inc(params_psum, 1)
            pe.wait_ge(tokens_here, 80)
            for k in range(DK):
                if k >= 4:
                    pe.wait_ge(xT_ready, k - 3)
                for i, (t0, n) in enumerate(TILES):
                    ins = nc.tensor.transpose(bank[1 + k % 4][:, t0:t0 + n], xtok_in[0:n, i, 128 * k:128 * k + 128], ident[0:n, 0:n])
                ins.then_inc(xin_psum, 1)

            for l in range(LAYERS):
                s0 = FIRST[l]
                norm_sums(2 * l)
                pe.wait_ge(conv_rows_here, 16 * (l + 1))
                pe.wait_ge(xT_ready, 8 if l == 0 else 24)
                for k in range(DK):
                    ins = nc.tensor.transpose(bank[1][:, 24 * k:24 * k + 24], tails[0:24, 128 * k:128 * k + 128], ident[0:24, 0:24])
                ins.then_inc(prev_psum, 1)
                pe.wait_ge(prev_ready, l + 1)
                pe.wait_ge(hn_ready, 8 * (2 * l + 1))
                pe.wait_ge(dtw_here, 16 * (l + 1))

                def column_chunk(out, w, c0):
                    for k in range(DK):
                        ins = mm(out, w[:, k, c0:c0 + 128], hnT[:, k, :], start=(k == 0), stop=(k == DK - 1))
                        if k < DK - 1:
                            pay(ins)
                    return ins

                def sl(n):
                    return slab(s0 + n).rearrange("p (k n) -> p k n", k=DK)

                wait_slab(pe, s0)
                for i, (t0, n) in enumerate(TILES):
                    for k in range(DK):
                        mm(bank[1][0:n, 128 * i:128 * i + 128], hnT[:, k, t0:t0 + n], sl(0)[:, k, 128:256], start=(k == 0), stop=(k == DK - 1))
                for i, (t0, n) in enumerate(TILES):
                    for k in range(DK):
                        ins = mm(bank[1][0:n, 384 + 8 * i:392 + 8 * i], hnT[:, k, t0:t0 + n], wdt[:, k, :], start=(k == 0), stop=(k == DK - 1))
                ins.then_inc(proj_psum, 1)
                column_chunk(bank[2][:, 0:NT], sl(0), 0).then_inc(proj_psum, 1)
                owed[0] += 1
                for c in range(4):
                    wait_slab(pe, s0 + 1 + c // 2)
                    if c >= 2:
                        pe.wait_ge(proj_dve, 7 * l + (2 if c == 2 else 3))
                    column_chunk(bank[1 + (2 + c) % 4][:, 0:NT], sl(1 + c // 2), 128 * (c % 2)).then_inc(proj_psum, 1)
                    owed[0] += c % 2
                for step in range(8):
                    wait_slab(pe, s0 + 3 + step // 2)
                    n = 6 + step
                    if step < 4:
                        pe.wait_ge(proj_dve, 7 * l + 4 + step)
                    else:
                        pe.wait_ge(proj_raw, 8 * l + step - 3)
                    column_chunk(bank[1 + n % 4][:, 0:NT], sl(3 + step // 2), 128 * (step % 2)).then_inc(proj_psum, 1)
                    owed[0] += step % 2
                    if step < 5:
                        pe.wait_ge(qksq_ready, 5 * l + step + 1)
                        if step >= 2:
                            pe.wait_ge(qkrstd_ready, 5 * l + step - 1)
                        mm(bank[5 + step % 2][:, 0:NT], halves, tmp2[step % 2][:, 0, :], start=True, stop=True).then_inc(qksum_psum, 1)
                    if 1 <= step <= 5:
                        pe.wait_ge(qkn_ready, 5 * l + step)
                        if step >= 3:
                            pe.wait_ge(qk_ready, 5 * l + step - 2)
                        else:
                            pe.wait_ge(rstd_ready, 2 * l + 1)
                        mm(bank[(7, 0)[(step - 1) % 2]][:, 0:NT], turn, qk[:, step - 1, :], start=True, stop=True).then_inc(rot_psum, 1)
                for c in range(4):
                    wait_slab(pe, s0 + 7 + c // 2)
                    n = 14 + c
                    pe.wait_ge(proj_raw, 8 * l + 5 + c)
                    column_chunk(bank[1 + n % 4][:, 0:NT], sl(7 + c // 2), 128 * (c % 2)).then_inc(proj_psum, 1)
                    owed[0] += c % 2
                pe.wait_ge(qkrstd_ready, 5 * (l + 1))
                pe.wait_ge(tail_cols_ready, l + 1)
                for k in range(DK):
                    ins = nc.tensor.transpose(bank[5 + k // 4][0:27, 128 * (k % 4):128 * (k % 4) + 128],
                                              tail_cols[:, k, :], ident)
                    if k % 4 == 3:
                        ins.then_inc(tail_psum, 1)
                    else:
                        pay(ins)

                pe.wait_ge(dta_ready, l + 1)
                pe.wait_ge(tail_ready, 2 * (l + 1))
                for i, (t0, n) in enumerate(TILES):
                    mm(bank[6][0:8, UPPER[i][0]:NT], dta[0:n, i, :], upper[0:n, UOFF[i]:UOFF[i] + NT - t0], start=(i == 0), stop=(i == 2), skip_group_check=True)
                for j, (j0, nj) in enumerate(TILES):
                    for i in range(j + 1):
                        n = TILES[i][1]
                        c0 = UOFF[i] + j0 - UPPER[i][0]
                        mm(bank[5][0:nj, 8 * j:8 * j + 8], upper[0:n, c0:c0 + nj], dta[0:n, i, :], start=(i == 0), stop=(i == j))
                for j, (j0, nj) in enumerate(TILES):
                    for i in range(j, 3):
                        n = TILES[i][1]
                        c0 = LOFF[i] + j0
                        ins = mm(bank[5][0:nj, 24 + 8 * j:32 + 8 * j], lower[0:n, c0:c0 + nj], dta[0:n, i, :], start=(i == j), stop=(i == 2))
                ins.then_inc(cs_psum, 1)

                pe.wait_ge(xbc_ready, 8 * (l + 1))
                pe.wait_ge(proj_z, 4 * (l + 1))
                pe.wait_ge(qk_ready, 5 * (l + 1))
                for i, (t0, n) in enumerate(TILES):
                    for k in range(4):
                        ins = nc.tensor.transpose(bank[1 + i][0:n, 128 * k:128 * k + 128], xbc[:, k, t0:t0 + n], ident)
                    ins.then_inc(tok_psum, 1)
                for where, w0, k, i in ((4, 0, 4, 0), (4, 128, 5, 0), (4, 256, 4, 1), (4, 384, 5, 1), (7, 0, 4, 2), (7, 128, 5, 2)):
                    t0, n = TILES[i]
                    ins = nc.tensor.transpose(bank[where][0:n, w0:w0 + 128], xbc[:, k, t0:t0 + n], ident)
                    if w0 == 384 or (where == 7 and w0 == 128):
                        ins.then_inc(tok_psum, 1)
                for where, w0, i in ((7, 256, 0), (7, 384, 1), (0, 0, 2)):
                    t0, n = TILES[i]
                    nc.tensor.transpose(bank[where][0:n, w0:w0 + 128], qk[:, 0, t0:t0 + n], ident).then_inc(tok_psum, 1)

                def scores(hd):
                    c, g = hd // 2, hd % 2
                    h = slice(64 * g, 64 * g + 64)
                    A, B = (bank[1], bank[2]) if hd % 2 == 0 else (bank[3], bank[4])
                    if hd >= 2:
                        pe.wait_ge(negmax_ready, 8 * l + hd - 1)
                    q, k = qk[h, 1 + c, :], qk[h, 0, :]
                    mm(A[:, 0:128], q[:, 0:128], k[:, 0:128], start=True, stop=True)
                    mm(A[:, 128:384], q[:, 128:256], k[:, 0:256], start=True, stop=True)
                    mm(B[0:NP - 256, 0:NP], q[:, 256:NP], k[:, 0:NP], start=True, stop=True).then_inc(score_psum, 1)

                def attend(hd):
                    c, g = hd // 2, hd % 2
                    h = slice(64 * g, 64 * g + 64)
                    P, PT, T = attn[hd % 2][:, 0:656], attn[hd % 2][:, 656:1088], bank[5 + hd % 2]
                    pe.wait_ge(prob_ready, 8 * l + hd + 1)
                    if hd >= 2:
                        pe.wait_ge(probT_ready, 8 * l + hd - 1)
                    tr = nc.tensor.transpose
                    tr(T[:, 0:128], P[:, 0:128], ident)
                    tr(T[:, 128:256], P[:, 128:256], ident)
                    tr(T[:, 256:272], P[0:16, 384:512], ident[0:16, 0:16])
                    tr(T[:, 272:400], P[:, 256:384], ident)
                    tr(T[:, 400:416], P[0:16, 512:640], ident[0:16, 0:16])
                    tr(T[0:16, 416:432], P[0:16, 640:656], ident[0:16, 0:16]).then_inc(probT_psum, 1)
                    pe.wait_ge(probT_ready, 8 * l + hd + 1)
                    if g == 0 and c >= 2:
                        pe.wait_ge(att_ready, 4 * l + c - 1)
                    out = bank[(7, 0)[c % 2]]
                    mm(out[h, 0:NP], vtok[:, 0, h], PT[:, 0:272], start=True, stop=False)
                    mm(out[h, 128:NP], vtok[:, 1, h], PT[:, 272:416], start=False, stop=False)
                    ins = mm(out[h, 256:NP], vtok[0:16, 2, h], PT[0:16, 416:432], start=False, stop=True)
                    if g == 1:
                        ins.then_inc(att_psum, 1)

                pe.wait_ge(tok_ready, 8 * (l + 1))
                pe.wait_ge(cs_ready, l + 1)
                pe.wait_ge(wdec_ready, l + 1)
                scores(0)
                for hd in range(HEADS):
                    if hd + 1 < HEADS:
                        scores(hd + 1)
                    attend(hd)

                for half in range(2):
                    n = 2 * l + half
                    pe.wait_ge(caches_here, 64 * (n + 1))
                    if half == 0:
                        pe.wait_ge(negmax_ready, 8 * (l + 1))
                        pe.wait_ge(probT_ready, 8 * (l + 1))
                    else:
                        pe.wait_ge(s_probT_ready, n)
                    for b in range(4):
                        nc.tensor.transpose(bank[1][:, 128 * b:128 * b + 128], winK[:, b, :], ident)
                    nc.tensor.transpose(bank[2][:, 0:64], metK[0:64, :], ident[0:64, 0:64]).then_inc(s_KT_psum, 1)
                    pe.wait_ge(s_KT_ready, n + 1)
                    pe.wait_ge(qs_ready, l + 1)
                    for g in range(2):
                        h = slice(64 * g, 64 * g + 64)
                        for b in range(4):
                            t0 = NP + 8 * (4 * half + b)
                            q, r = qs[h, 4 * half + b, :, :].rearrange("p c t -> p (c t)"), slice(32 * b, 32 * b + 32)
                            out = bank[(3, 2)[g]][r, 0:152]
                            mm(out[:, 0:128], q, winKT[h, 128 * b:128 * b + 128], start=True, stop=True)
                            mm(out[:, 128:144], q, metKT[h, 16 * b:16 * b + 16], start=True, stop=True)
                            ins = mm(out[:, 144:152], q, qk[h, 0, t0:t0 + ST], start=True, stop=True)
                    ins.then_inc(s_score_psum, 1)
                    pe.wait_ge(s_prob_ready, n + 1)
                    for g in range(2):
                        nc.tensor.transpose(bank[4][:, 128 * g:128 * g + 128], sprob[:, g, 0:128], ident)
                        ins = nc.tensor.transpose(bank[4][0:24, 256 + 128 * g:384 + 128 * g], sprob[:, g, 128:152], ident)
                    ins.then_inc(s_probT_psum, 1)
                    pe.wait_ge(s_probT_ready, n + 1)
                    pe.wait_ge(mnv_new_here, 64 * (n + 1))
                    if half:
                        pe.wait_ge(s_att_ready, n)
                    for b in range(4):
                        for g in range(2):
                            h = slice(64 * g, 64 * g + 64)
                            cols = slice(32 * b, 32 * b + 32)
                            mm(bank[5][h, cols], winV[:, b, h], sprobT[:, 128 * g + 32 * b:128 * g + 32 * b + 32], start=True, stop=False)
                            ins = mm(bank[5][h, cols], mnV[0:24, b, h], sprobT[0:24, 256 + 128 * g + 32 * b:256 + 128 * g + 32 * b + 32], start=False, stop=True)
                    ins.then_inc(s_att_psum, 1)
                pe.wait_ge(mixsq_ready, 3 * l + 1)
                for c in range(4):
                    ins = mm(bank[6][:, 0:NT], ones[:, :], conv[:, c, 0:NT], start=(c == 0), stop=(c == 3))
                ins.then_inc(mixsum_psum, 1)

                pe.wait_ge(s_KT_ready, 2 * (l + 1))
                for g in range(2):
                    Bc, Cc = 4 + g, 6 + g
                    if g:
                        pe.wait_ge(h0T_ready, 2 * (4 * l + 2))
                    for j, (j0, nj) in enumerate(TILES):
                        out = bank[1][0:nj, 0:NT] if j == 0 else bank[2][0:nj, UOFF[j] - NT:UOFF[j] - NT + NT - j0]
                        ins = mm(out, xbc[:, Bc, j0:j0 + nj], xbc[:, Cc, j0:NT], start=True, stop=True)
                    ins.then_inc(cb_psum, 1)
                    for pr in (2 * g, 2 * g + 1):
                        n = 4 * l + pr
                        for hh in range(2):
                            h = 2 * pr + hh
                            if h >= 2:
                                pe.wait_ge(seg_ready, 8 * l + h - 1)
                            else:
                                pe.wait_ge(s_probT_ready, 2 * (l + 1))
                            mm(bank[3 + h % 2][:, 0:NT], ident[0:8, h:h + 1].to_broadcast([8, 128]), csrow, start=True, stop=True).then_inc(seg_psum, 1)
                        pe.wait_ge(cb_ready, 2 * l + g + 1)
                        if pr % 2:
                            pe.wait_ge(h0T_ready, 2 * n)
                        pe.wait_ge(h0_here, 16 * (n + 1))
                        for b in range(SB):
                            ins = nc.tensor.transpose(bank[1 + b // 4][:, 128 * (b % 4):128 * (b % 4) + 128], h0[:, b, :], ident)
                            if b % 4 == 3:
                                ins.then_inc(h0T_psum, 1)
                        if pr:
                            pe.wait_ge(y_ready, 3 * l * 4 + 3 * pr)
                            pe.wait_ge(pstate_ready, n)
                        else:
                            pe.wait_ge(att_ready, 4 * (l + 1))
                        for hh in range(2):
                            h = 2 * pr + hh
                            mm(bank[7][64 * hh:64 * hh + 64, 0:64], ident[0:8, h:h + 1].to_broadcast([8, 64]), csrow[:, NP:NT], start=True, stop=True)
                        pe.wait_ge(h0T_ready, 2 * (n + 1))
                        for b in range(SB):
                            ins = mm(bank[7][:, 64 + 8 * b:72 + 8 * b], h0T[:, b, :], xbc[:, Cc, NP + 8 * b:NP + 8 * b + 8], start=True, stop=True)
                        ins.then_inc(yoff_psum, 1)
                        if pr >= 2:
                            pe.wait_ge(y_ready, 3 * (4 * l + pr - 1))
                        elif pr == 0:
                            pe.wait_ge(s_att_ready, 2 * (l + 1))
                        else:
                            pe.wait_ge(mixrstd_ready, 3 * l + 1)
                        for hh in range(2):
                            h = 2 * pr + hh
                            pe.wait_ge(M_ready, 8 * l + h + 1)
                            for j, (j0, nj) in enumerate(TILES):
                                ins = mm(bank[5 + pr % 2][64 * hh:64 * hh + 64, j0:NT], xdt[0:nj, j, 64 * h:64 * h + 64],
                                         decay[h % 2][0:nj, UOFF[j]:UOFF[j] + NT - j0], start=(j == 0), stop=(j == 2))
                        ins.then_inc(ydiag_psum, 1)
                        pe.wait_ge(xw_ready, n + 1)
                        pe.wait_ge(y_ready, 3 * n + 1)
                        for j, nj in ((0, 128), (1, 128), (2, NP - 256)):
                            ins = mm(bank[7][:, 128:256], xw[0:nj, j, :], Btok[0:nj, j, 128 * g:128 * g + 128], start=(j == 0), stop=(j == 2))
                        ins.then_inc(pstate_psum, 1)
                        pe.wait_ge(Bexp_ready, 2 * l + g + 1)
                        for q in range(2):
                            pe.wait_ge(sstate_ready, 2 * n + q) if (n or q) else None
                            mm(bank[0][:, :], xw[0:80, 2, :], Bexp[0:80, 4 * q:4 * q + 4, :], start=True, stop=True).then_inc(sstate_psum, 1)
                for g in range(2):
                    pe.wait_ge(mixsq_ready, 3 * l + 2 + g)
                    for c in (2 * g, 2 * g + 1):
                        ins = mm(bank[1 + g][:, 0:NT], ones[:, :], conv[:, 4 + c, 0:NT], start=(c % 2 == 0), stop=(c % 2 == 1))
                    ins.then_inc(mixsum_psum, 1)
                pe.wait_ge(mix_ready, 8 * (l + 1))
                for i in range(DK):
                    wait_slab(pe, s0 + IN_SLABS + i // 2)
                    w = sl(IN_SLABS + i // 2)
                    if i >= 4:
                        pe.wait_ge(xT_ready, 8 + 16 * l + i - 3)
                    for k in range(DK):
                        ins = mm(bank[3 + i % 4][:, 0:NT], w[:, k, 128 * (i % 2):128 * (i % 2) + 128], mixT[:, k, :], start=(k == 0), stop=(k == DK - 1))
                        if k < DK - 1:
                            pay(ins)
                    ins.then_inc(out_psum, 1)
                    owed[0] += i % 2

                norm_sums(2 * l + 1)
                pe.wait_ge(hn_ready, 8 * (2 * l + 2))
                if l == 0:
                    f0 = IN_SLABS + OUT_SLABS
                    for f in range(FC):
                        for w in range(2):
                            n = f0 + 2 * (f // 2) + w
                            wait_slab(pe, n)
                            s = slab(n).rearrange("p (k n) -> p k n", k=DK)
                            if f >= 2:
                                pe.wait_ge(hid_ready, f - 1)
                            else:
                                pe.wait_ge(xT_ready, 16)
                            for k in range(DK):
                                ins = mm(bank[1 + 2 * w + f % 2][:, 0:NT], s[:, k, 128 * (f % 2):128 * (f % 2) + 128], hnT[:, k, :], start=(k == 0), stop=(k == DK - 1))
                                if k < DK - 1:
                                    pay(ins)
                            ins.then_inc(gu_psum, 1)
                            owed[0] += f % 2
                    for half in range(2):
                        for f in range(FC):
                            blk = half * FC + f
                            n = f0 + GU_SLABS + blk // 4
                            wait_slab(pe, n)
                            s = slab(n).rearrange("p (j n) -> p j n", j=4)[:, blk % 4, :]
                            pe.wait_ge(hid_ready, f + 1)
                            for i in range(4):
                                if half and f == 0:
                                    pe.wait_ge(xT_ready, 16 + i + 1)
                                ins = mm(bank[(5, 6, 7, 0)[i]][:, 0:NT], s[:, 128 * i:128 * i + 128], hidT[:, f, :], start=(f == 0), stop=(f == FC - 1))
                                if f == FC - 1:
                                    ins.then_inc(down_psum, 1)
                                else:
                                    pay(ins)
                            owed[0] += blk % 4 == 3

            pe.wait_ge(router_here, 16)
            for i, (t0, n) in enumerate(TILES):
                for k in range(DK):
                    ins = mm(bank[1][0:n, 8 * i:8 * i + 8], hnT[:, k, t0:t0 + n], wr[:, k, :], start=(k == 0), stop=(k == DK - 1))
            ins.then_inc(logit_psum, 1)
            pe.wait_ge(xT_ready, 32)
            for src, done, signal in ((hnT, None, turn_psum), (xT, turn_act, comb_psum)):
                for u in range(6):
                    i, half = u // 2, u % 2
                    t0, n = TILES[i]
                    if done is not None:
                        pe.wait_ge(done, u + 1)
                    for q in range(4):
                        ins = nc.tensor.transpose(bank[2 + u][0:n, 128 * q:128 * q + 128], src[:, 4 * half + q, t0:t0 + n], ident)
                    ins.then_inc(signal, 1)
            pe.wait_ge(picks_counted, 1)
            m = R(0)
            for j in range(3):
                nj = TILES[j][1]
                for i in range(j + 1):
                    n = TILES[i][1]
                    tri = upper[0:n, UOFF[1]:UOFF[1] + nj] if i == j else ones[0:n, 0:nj]
                    mm(bank[1][0:nj, 32 + 8 * j:40 + 8 * j], tri, m[0:n, i, :], start=(i == 0), stop=(i == j))
            for i in range(3):
                n = TILES[i][1]
                ins = mm(bank[1][:, 64:72], ones[0:n, :], m[0:n, i, :], start=(i == 0), stop=(i == 2))
            ins.then_inc(count_psum, 1)
            pe.wait_ge(comb_added, 6)
            pe.wait_ge(route_ready, 1)

            def gather(k):
                pe.wait_ge(pick_ready, k + 1)
                for c in range(DK):
                    for i, (t0, n) in enumerate(TILES):
                        ins = mm(bank[c // 4][:, 128 * (c % 4):128 * (c % 4) + 128], hn_tok[0:n, i, 128 * c:128 * c + 128], pick[0:n, i, :], start=(i == 0), stop=(i == 2))
                        if i < 2:
                            pay(ins)
                    if c % 4 == 3:
                        ins.then_inc(xg_psum, 1)
                if k is not first_pass:
                    pe.wait_ge(pickT_ready, k)
                for i, (t0, n) in enumerate(TILES):
                    ins = nc.tensor.transpose(bank[2][:, t0:t0 + n], gpick[0:n, i, :], ident[0:n, 0:n])
                ins.then_inc(pickT_psum, 1)

            def expert_pass(k):
                pe.wait_ge(xg_ready, 2 * k + 2)
                for f in range(FC):
                    for w in range(2):
                        j = 2 * (f // 2) + w
                        s = (MOE0 + j) % RING
                        if f % 2 == 0:
                            pe.wait_ge(slab_here[s], k * (16 * FFN_SLABS // RING) + (fixed_seen[s] + 16 * (j // RING + 1)))
                        if w == 0:
                            pe.wait_ge(hid_ready, k * FC + (FC + f - 1))
                        for c in range(DK):
                            ins = mm(bank[3 + f % 2][:, 128 * w:128 * w + 128], slots[s].rearrange("p (k n) -> p k n", k=DK)[:, c, 128 * (f % 2):128 * (f % 2) + 128],
                                     xg[:, c, :], start=(c == 0), stop=(c == DK - 1))
                            if c < DK - 1:
                                pay(ins)
                        owed[0] += f % 2
                        if w == 1:
                            ins.then_inc(gu_psum, 1)
                for f in range(FC):
                    j = GU_SLABS + f // 2
                    s = (MOE0 + j) % RING
                    if f % 2 == 0:
                        pe.wait_ge(slab_here[s], k * (16 * FFN_SLABS // RING) + (fixed_seen[s] + 16 * (j // RING + 1)))
                    pe.wait_ge(hid_ready, k * FC + (FC + f + 1))
                    if f == 0:
                        pe.wait_ge(comb_added, 6 * k + 6)
                    for half in range(2):
                        ins = mm(bank[5 + half][:, :], hid[:, f, :], slots[s].rearrange("p (r n) -> p r n", r=2)[:, f % 2, 512 * half:512 * half + 512],
                                 start=(f == 0), stop=(f == FC - 1))
                        if f == FC - 1:
                            ins.then_inc(y_psum, 1)
                        else:
                            pay(ins)
                    owed[0] += f % 2
                pe.wait_ge(pickT_ready, k + 1)
                gather(k + 1)
                pe.wait_ge(ytok_ready, 2 * k + 2)
                for u in range(6):
                    i, half = u // 2, u % 2
                    t0, n = TILES[i]
                    if u >= 3:
                        pe.wait_ge(comb_added, 6 * k + (u + 4))
                    mm(bank[5 + u % 3][0:n, :], gpickT[:, t0:t0 + n], ytok[:, 512 * half:512 * half + 512], start=True, stop=True).then_inc(comb_psum, 1)
                assert owed[0] == 0

            gather(first_pass)
            with pe.Fori(0, EXPERTS) as e:
                expert_pass(e)
            fullest = pe.value_load(crowded[0:1, 0:1], min_val=0, max_val=NT)
            with pe.If(fullest > SLOTS):
                with pe.Fori(1, PASSES) as b:
                    with pe.Fori(0, EXPERTS) as e:
                        expert_pass(b * EXPERTS + e)

        @block.scalar
        def _(act):
            step = [0]

            def link(ins):
                step[0] += 1
                ins.then_inc(act_step, 1)
                act.wait_ge(act_step, step[0])

            f = nc.scalar.activation
            act.wait_ge(set_up, 3)

            def norm(n, out):
                act.wait_ge(xT_ready, 8 * (n + 1))
                f(hnT_[:, :], xT_[:, :], ACT.Square).then_inc(squares_ready, 1)
                act.wait_ge(sum_psum, n + 1)
                link(f(out, bank[0][:, 0:NT], ACT.Ln, scale=1.0 / D, bias=eps))
                f(out, out, ACT.Exp, scale=-0.5).then_inc(rstd_ready, 1)

            for l in range(LAYERS):
                if l:
                    act.wait_ge(down_psum, 8)
                    act.wait_ge(hid_ready, FC)
                norm(2 * l, rstd)
                for s in range(8):
                    if s < 5:
                        act.wait_ge(proj_dve, 7 * l + 3 + s)
                        if s >= 2:
                            act.wait_ge(qk_ready, 5 * l + s - 1)
                        t = tmp2[s % 2]
                        f(t[:, 0, :], qk[:, s, :], ACT.Square).then_inc(qksq_ready, 1)
                    act.wait_ge(proj_psum, 18 * l + 7 + s)
                    if s == 0:
                        act.wait_ge(prev_ready, l + 1)
                    src = bank[1 + (6 + s) % 4]
                    f(raw[:, s, 3:NP + 3], src[:, 0:NP], ACT.Copy)
                    f(raw[:, s, S0:NPAD].rearrange("p (b t) -> p b t", t=ST + 3)[:, :, 3:ST + 3],
                      src[:, NP:NT].rearrange("p (b t) -> p b t", t=ST), ACT.Copy).then_inc(proj_raw, 1)
                    if s < 5:
                        act.wait_ge(qksum_psum, 5 * l + s + 1)
                        link(f(t[:, 1, :], bank[5 + s % 2][:, 0:NT], ACT.Ln, scale=1.0 / 64, bias=eps))
                        f(t[:, 1, :], t[:, 1, :], ACT.Exp, scale=-0.5).then_inc(qkrstd_ready, 1)
                act.wait_ge(dt_exp_in, l + 1)
                f(nega, alog[l], ACT.Exp)
                f(dw[1], dw[1], ACT.Exp, scale=-1.0).then_inc(dt_exp, 1)
                act.wait_ge(dt_ln_in, l + 1)
                f(dw[3], dw[2], ACT.Ln).then_inc(dt_ln, 1)
                for c in range(4):
                    act.wait_ge(proj_psum, 18 * l + 15 + c)
                    f(zs[:, c, :], bank[1 + (14 + c) % 4][:, 0:NT], ACT.Silu).then_inc(proj_z, 1)
                act.wait_ge(conv_ready, 8 * (l + 1))
                act.wait_ge(tail_psum, 2 * (l + 1))
                for k in range(DK):
                    f(xbc[:, k, 0:NP], conv[:, k, 0:NP], ACT.Silu)
                    f(xbc[:, k, NP:NT].rearrange("p (b t) -> p b t", t=ST),
                      samples_of_conv(conv, k), ACT.Silu).then_inc(xbc_ready, 1)
                act.wait_ge(cs_psum, l + 1)
                act.wait_ge(cs_ready, l + 1)
                f(wdec[:, 0:2, :], bank[5][:, 24:40].rearrange("p (i h) -> p i h", i=2), ACT.Exp)
                f(wdec[0:80, 2, :], bank[5][0:80, 40:48], ACT.Exp).then_inc(wdec_ready, 1)
                for hd in range(HEADS):
                    c, g, n = hd // 2, hd % 2, 8 * l + hd
                    P, i = attn[hd % 2][:, 0:656], hd % 2
                    act.wait_ge(negmax_ready, n + 1)
                    sink = sinks[l][:, c + 4 * g:c + 4 * g + 1]
                    f(es[i], nm[i], ACT.Exp, bias=sink)
                    f(P[:, 0:128], P[:, 0:128], ACT.Exp, bias=nm[i][:, 0:1], accum_out=sums[i][:, 0:1])
                    f(P[:, 128:384], P[:, 128:384], ACT.Exp, bias=nm[i][:, 1:2], accum_out=sums[i][:, 1:2])
                    f(P[0:16, 384:656], P[0:16, 384:656], ACT.Exp, bias=nm[i][0:16, 2:3], accum_out=sums[i][0:16, 2:3]).then_inc(exp_ready, 1)
                for half in range(2):
                    n = 2 * l + half
                    act.wait_ge(s_negmax_ready, n + 1)
                    for g in range(2):
                        f(es[0][:, g:g + 1], nm[0][:, g:g + 1], ACT.Exp, bias=sink_s[l][:, g:g + 1])
                        ins = f(sprob[:, g, :], sprob[:, g, :], ACT.Exp, bias=nm[0][:, g:g + 1], accum_out=sums[0][:, g:g + 1])
                    ins.then_inc(s_exp_ready, 1)

                act.wait_ge(att_ready, 4 * (l + 1))
                act.wait_ge(s_att_ready, 2 * (l + 1))
                act.wait_ge(att_psum, 4 * (l + 1))
                f(conv[:, 0:4, 0:NT], mixT[:, 4:8, :], ACT.Square).then_inc(mixsq_ready, 1)
                act.wait_ge(mixsum_psum, 3 * l + 1)
                link(f(rstd_m, bank[6][:, 0:NT], ACT.Ln, scale=1.0 / 512, bias=eps))
                f(rstd_m, rstd_m, ACT.Exp, scale=-0.5).then_inc(mixrstd_ready, 1)
                for pr in range(4):
                    n = 4 * l + pr
                    for h in (2 * pr, 2 * pr + 1):
                        act.wait_ge(seg_ready, 8 * l + h + 1)
                        f(decay[h % 2][:, 0:UOFF[2]], decay[h % 2][:, 0:UOFF[2]], ACT.Exp)
                        f(decay[h % 2][0:80, UOFF[2]:UCOLS], decay[h % 2][0:80, UOFF[2]:UCOLS], ACT.Exp).then_inc(decay_exp, 1)
                    act.wait_ge(yoff_psum, n + 1)
                    if n:
                        act.wait_ge(sstate_ready, 2 * n)
                        act.wait_ge(y_ready, 3 * n)
                    f(eoff, bank[7][:, 0:64], ACT.Exp).then_inc(eoff_ready, 1)
                for g in range(2):
                    act.wait_ge(y_ready, 12 * (l + 1))
                    act.wait_ge(mixsum_psum, 3 * l + 1 + g)
                    f(conv[:, 4 + 2 * g:6 + 2 * g, 0:NT], mixT[:, 2 * g:2 * g + 2, :], ACT.Square).then_inc(mixsq_ready, 1)
                    act.wait_ge(mixsum_psum, 3 * l + 2 + g)
                    act.wait_ge(mix_ready, 8 * l + 4 + 2 * g)
                    link(f(rstd_m, bank[1 + g][:, 0:NT], ACT.Ln, scale=1.0 / 256, bias=eps))
                    f(rstd_m, rstd_m, ACT.Exp, scale=-0.5).then_inc(mixrstd_ready, 1)
                act.wait_ge(out_psum, 8 * (l + 1))
                norm(2 * l + 1, rstd_f)
                if l == 0:
                    for c in range(FC):
                        act.wait_ge(gu_psum, 2 * c + 1)
                        if c >= 2:
                            act.wait_ge(hid_ready, c - 1)
                        f(gate_s[c % 2], bank[1 + c % 2][:, 0:NT], ACT.Silu).then_inc(silu_ready, 1)
            act.wait_ge(gates_in, 1)
            f(R(96, 3, 1)[:, :, 0], R(96, 3, 1)[:, :, 0], ACT.Exp).then_inc(gates_exp, 1)
            for u in range(6):
                i, half = u // 2, u % 2
                n = TILES[i][1]
                act.wait_ge(turn_psum, u + 1)
                f(hn_tok[0:n, i, 512 * half:512 * half + 512], bank[2 + u][0:n, :], ACT.Copy).then_inc(turn_act, 1)

            def gathered(k):
                for half in range(2):
                    act.wait_ge(xg_psum, 2 * k + (half + 1))
                    f(xg_[:, 512 * half:512 * half + 512], bank[half][:, :], ACT.Copy).then_inc(xg_ready, 1)

            def expert_pass(k):
                for c in range(FC):
                    act.wait_ge(gu_psum, k * FC + (2 * FC + c + 1))
                    act.wait_ge(hid_ready, k * FC + (FC + c - 1))
                    f(gsil[c % 2], bank[3 + c % 2][:, 0:128], ACT.Silu).then_inc(silu_ready, 1)
                act.wait_ge(comb_psum, 6 * k + 6)
                for half in range(2):
                    act.wait_ge(y_psum, 2 * k + (half + 1))
                    f(ytok[:, 512 * half:512 * half + 512], bank[5 + half][:, :], ACT.Copy).then_inc(ytok_ready, 1)
                gathered(k + 1)

            act.wait_ge(route_ready, 1)
            gathered(0)
            with act.Fori(0, EXPERTS) as e:
                expert_pass(e)
            fullest = act.value_load(crowded[0:1, 0:1], min_val=0, max_val=NT)
            with act.If(fullest > SLOTS):
                with act.Fori(1, PASSES) as b:
                    with act.Fori(0, EXPERTS) as e:
                        expert_pass(b * EXPERTS + e)

        @block.vector
        def _(dve):
            v = nc.vector
            step = [0]

            def link(ins):
                step[0] += 1
                ins.then_inc(dve_step, 1)
                dve.wait_ge(dve_step, step[0])

            dve.wait_ge(set_up, 3)
            dve.wait_ge(const_here, 16)
            dve.wait_ge(small_here, 16 * 25 * LAYERS)
            dve.wait_ge(params_psum, 1)
            link(v.tensor_copy(params[:, :], bank[7][:, 0:128]))
            for l in range(LAYERS):
                link(v.tensor_scalar(qkw[2 * l + 1], qkw[2 * l + 1], 0.125, None, ALU.mult))
            for k in range(DK):
                dve.wait_ge(xin_psum, k + 1)
                v.tensor_copy(xT[:, k, :], bank[1 + k % 4][:, 0:NT]).then_inc(xT_ready, 1)

            def normed(n, l, r0, scale):
                dve.wait_ge(rstd_ready, n + 1)
                for k in range(DK):
                    c = PARAM_ROWS * l + r0 + k
                    v.scalar_tensor_tensor(out=hnT[:, k, :], in0=xT[:, k, :], scalar=params[:, c:c + 1], in1=scale,
                                           op0=ALU.mult, op1=ALU.mult).then_inc(hn_ready, 1)

            for l in range(LAYERS):
                P0 = PARAM_ROWS * l
                if l:
                    dve.wait_ge(down_psum, 8)
                dve.wait_ge(xT_ready, 8 if l == 0 else 24)
                link(v.memset(raw[:, :, 0:3], 0.0))
                dve.wait_ge(prev_psum, l + 1)
                for r in range(3):
                    ins = v.tensor_copy(raw[:, :, S0 + r:S0 + r + 78:11], bank[1][:, 0:192].rearrange("p (k b r) -> p k b r", k=DK, r=3)[:, :, :, r])
                    (ins.then_inc(prev_ready, 1) if r == 2 else None)
                normed(2 * l, l, R_MIX, rstd)
                dve.wait_ge(proj_psum, 18 * l + 1)
                v.tensor_copy(vtok[:, 0:2, :], bank[1][:, 0:256].rearrange("p (i n) -> p i n", i=2))
                v.tensor_copy(vtok[0:80, 2, :], bank[1][0:80, 256:384]).then_inc(proj_dve, 1)
                raw_dt = dw[0]
                v3 = [w.rearrange("p (i h) -> p i h", i=3) for w in dw]
                v.tensor_tensor(v3[0][:, 0:2, :], bank[1][:, 384:400].rearrange("p (i h) -> p i h", i=2), bc(dtb[l], 1, 2), ALU.add)
                v.tensor_tensor(v3[0][0:80, 2, :], bank[1][0:80, 400:408], dtb[l][0:80, :], ALU.add).then_inc(proj_dve, 1)
                for n in range(5):
                    dve.wait_ge(proj_psum, 18 * l + 2 + n)
                    v.tensor_copy(qk[:, n, :], bank[1 + (1 + n) % 4][:, 0:NT]).then_inc(proj_dve, 1)
                dve.wait_ge(proj_dve, 7 * l + 7)
                link(v.tensor_scalar(dw[1], raw_dt, -1.0, None, ALU.mult))
                v.tensor_tensor(dw[1], dw[1], raw_dt, ALU.max).then_inc(dt_exp_in, 1)

                def conv_chunk(k):
                    dve.wait_ge(proj_raw, 8 * l + k + 1)
                    for w in range(CONV_W):
                        s = params[:, P0 + R_CW + 8 * w + k:P0 + R_CW + 8 * w + k + 1]
                        if w == 0:
                            link(v.tensor_scalar(conv[:, k, 0:NCONV], raw[:, k, 0:NCONV], s, params[:, P0 + R_CB + k:P0 + R_CB + k + 1], ALU.mult, ALU.add))
                        else:
                            ins = v.scalar_tensor_tensor(out=conv[:, k, 0:NCONV], in0=raw[:, k, w:w + NCONV], scalar=s, in1=conv[:, k, 0:NCONV], op0=ALU.mult, op1=ALU.add)
                            if w < CONV_W - 1:
                                link(ins)
                            else:
                                ins.then_inc(conv_ready, 1)

                def turned(n):
                    t = tmp2[n % 2]
                    dve.wait_ge(rot_psum, 5 * l + n + 1)
                    link(v.tensor_tensor(t[:, 2, :], bank[(7, 0)[n % 2]][:, 0:NT], sinT, ALU.mult))
                    link(v.tensor_tensor(qk[:, n, :], qk[:, n, :], cosT, ALU.mult))
                    v.tensor_tensor(qk[:, n, :], qk[:, n, :], t[:, 2, :], ALU.add).then_inc(qk_ready, 1)

                if l:
                    pass
                for s in range(8):
                    if s < 5:
                        dve.wait_ge(qkrstd_ready, 5 * l + s + 1)
                        w = qkw[2 * l + (1 if s else 0)]
                        v.scalar_tensor_tensor(out=qk[:, s, :], in0=qk[:, s, :], scalar=w, in1=tmp2[s % 2][:, 1, :], op0=ALU.mult, op1=ALU.mult).then_inc(qkn_ready, 1)
                    conv_chunk(s)
                    if 1 <= s <= 5:
                        turned(s - 1)
                for k in range(DK):
                    ins = v.tensor_copy(tail_cols[:, k, :].rearrange("p (j r) -> p j r", r=3), tail_view(raw, k))
                ins.then_inc(tail_cols_ready, 1)
                dve.wait_ge(qk_ready, 5 * (l + 1))
                for c in range(4):
                    ins = v.tensor_copy(qs[:, :, c, :], qk[:, 1 + c, NP:NT].rearrange("p (b t) -> p b t", t=ST))
                ins.then_inc(qs_ready, 1)
                dve.wait_ge(dt_exp, l + 1)
                v.tensor_scalar(dw[2], dw[1], 1.0, None, ALU.add).then_inc(dt_ln_in, 1)
                dve.wait_ge(dt_ln_in, l + 1)
                link(v.tensor_scalar(dw[4], dw[2], -1.0, 1e-30, ALU.add, ALU.max))
                link(v.reciprocal(dw[4], dw[4]))
                link(v.tensor_tensor(dw[4], dw[4], dw[1], ALU.mult))
                dve.wait_ge(dt_ln, l + 1)
                link(v.tensor_tensor(dw[4], dw[4], dw[3], ALU.mult))
                link(v.tensor_scalar(dw[3], dw[2], 1.0, None, ALU.is_equal))
                link(v.tensor_tensor(dw[3], dw[3], dw[1], ALU.mult))
                link(v.tensor_tensor(dw[4], dw[4], dw[3], ALU.add))
                link(v.scalar_tensor_tensor(out=dt.rearrange("p i h -> p (i h)"), in0=raw_dt, scalar=0.0, in1=dw[4], op0=ALU.max, op1=ALU.add))
                link(v.tensor_tensor(dta, dt, bc(nega, 1, 3), ALU.mult))
                v.tensor_scalar(dta, dta, -1.0, None, ALU.mult).then_inc(dta_ready, 1)
                for h in range(2):
                    dve.wait_ge(tail_psum, 2 * l + h + 1)
                    v.tensor_copy(tails[0:27, 512 * h:512 * h + 512], bank[5 + h][0:27, :]).then_inc(tail_ready, 1)
                dve.wait_ge(cs_psum, l + 1)
                v.tensor_copy(csrow, bank[6][0:8, 0:NT])
                v.tensor_scalar(negcs[:, 0:2, :], bank[5][:, 0:16].rearrange("p (i h) -> p i h", i=2), -1.0, None, ALU.mult)
                v.tensor_scalar(negcs[0:80, 2, :], bank[5][0:80, 16:24], -1.0, None, ALU.mult).then_inc(cs_ready, 1)
                for i, (t0, n) in enumerate(TILES):
                    dve.wait_ge(tok_psum, 8 * l + i + 1)
                    v.tensor_tensor(xdt[0:n, i, :].rearrange("p (h d) -> p h d", h=HEADS), bank[1 + i][0:n, :].rearrange("p (h d) -> p h d", h=HEADS),
                                    bc(dt[0:n, i, :], 2, 64), ALU.mult).then_inc(tok_ready, 1)
                dve.wait_ge(tok_psum, 8 * l + 4)
                v.tensor_copy(Btok[:, 0:2, :], bank[4][:, :].rearrange("p (i n) -> p i n", i=2)).then_inc(tok_ready, 1)
                dve.wait_ge(tok_psum, 8 * l + 7)
                v.tensor_copy(Btok[0:80, 2, :], bank[7][0:80, 0:256]).then_inc(tok_ready, 1)
                for n, (src, i) in enumerate(((bank[7][:, 256:384], 0), (bank[7][:, 384:512], 1), (bank[0][0:80, 0:128], 2))):
                    dve.wait_ge(tok_psum, 8 * l + 6 + n)
                    v.tensor_copy(ktok[0:src.shape[0], i, :], src).then_inc(tok_ready, 1)

                def masked(hd):
                    c, g, i = hd // 2, hd % 2, hd % 2
                    A, B = (bank[1], bank[2]) if i == 0 else (bank[3], bank[4])
                    P = attn[i][:, 0:656]
                    dve.wait_ge(score_psum, 8 * l + hd + 1)
                    if hd >= 2:
                        dve.wait_ge(probT_psum, 8 * l + hd - 1)
                    v.tensor_tensor(P[:, 0:128], A[:, 0:128], C("mask0"), ALU.add)
                    v.tensor_tensor(P[:, 128:384], A[:, 128:384], C("mask1"), ALU.add)
                    link(v.tensor_tensor(P[0:16, 384:656], B[0:16, 0:NP], C("mask2")[0:16, :], ALU.add))
                    v.tensor_reduce(mx[i][:, 0:1], P[:, 0:128], AX.X, ALU.max)
                    v.tensor_reduce(mx[i][:, 1:2], P[:, 128:384], AX.X, ALU.max)
                    link(v.tensor_reduce(mx[i][0:16, 2:3], P[0:16, 384:656], AX.X, ALU.max))
                    v.tensor_scalar(nm[i], mx[i], sinks[l][:, c + 4 * g:c + 4 * g + 1], -1.0, ALU.max, ALU.mult).then_inc(negmax_ready, 1)

                def probs(hd):
                    i = hd % 2
                    P = attn[i][:, 0:656]
                    dve.wait_ge(exp_ready, 8 * l + hd + 1)
                    link(v.tensor_tensor(sums[i], sums[i], es[i], ALU.add))
                    link(v.reciprocal(sums[i], sums[i]))
                    v.tensor_scalar(P[:, 0:128], P[:, 0:128], sums[i][:, 0:1], None, ALU.mult)
                    v.tensor_scalar(P[:, 128:384], P[:, 128:384], sums[i][:, 1:2], None, ALU.mult)
                    v.tensor_scalar(P[0:16, 384:656], P[0:16, 384:656], sums[i][0:16, 2:3], None, ALU.mult).then_inc(prob_ready, 1)

                def probsT(hd):
                    PT, T = attn[hd % 2][:, 656:1088], bank[5 + hd % 2]
                    dve.wait_ge(probT_psum, 8 * l + hd + 1)
                    v.tensor_copy(PT[:, 0:416], T[:, 0:416])
                    v.tensor_copy(PT[0:16, 416:432], T[0:16, 416:432]).then_inc(probT_ready, 1)

                dve.wait_ge(proj_psum, 18 * (l + 1))
                dve.wait_ge(xbc_ready, 8 * (l + 1))
                masked(0)
                for hd in range(HEADS):
                    if hd + 1 < HEADS:
                        masked(hd + 1)
                    probs(hd)
                    probsT(hd)
                    if hd % 2 == 1:
                        c = hd // 2
                        dve.wait_ge(att_psum, 4 * l + c + 1)
                        v.tensor_copy(mixT[:, 4 + c, 0:NP], bank[(7, 0)[c % 2]][:, 0:NP]).then_inc(att_ready, 1)
                for half in range(2):
                    n = 2 * l + half
                    dve.wait_ge(s_KT_psum, n + 1)
                    v.tensor_copy(winKT, bank[1][:, :])
                    v.tensor_copy(metKT, bank[2][:, 0:64]).then_inc(s_KT_ready, 1)
                    dve.wait_ge(s_score_psum, n + 1)
                    v.tensor_tensor(sprob[:, 0, :], bank[3][:, 0:152], C("mask_s"), ALU.add)
                    link(v.tensor_tensor(sprob[:, 1, :], bank[2][:, 0:152], C("mask_s"), ALU.add))
                    link(v.tensor_reduce(mx[0][:, 0:2], sprob, AX.X, ALU.max))
                    link(v.tensor_tensor(mx[0][:, 0:2], mx[0][:, 0:2], sink_s[l], ALU.max))
                    v.tensor_scalar(nm[0][:, 0:2], mx[0][:, 0:2], -1.0, None, ALU.mult).then_inc(s_negmax_ready, 1)
                    dve.wait_ge(s_exp_ready, n + 1)
                    link(v.tensor_tensor(sums[0][:, 0:2], sums[0][:, 0:2], es[0][:, 0:2], ALU.add))
                    link(v.reciprocal(sums[0][:, 0:2], sums[0][:, 0:2]))
                    v.tensor_scalar(sprob[:, 0, :], sprob[:, 0, :], sums[0][:, 0:1], None, ALU.mult)
                    v.tensor_scalar(sprob[:, 1, :], sprob[:, 1, :], sums[0][:, 1:2], None, ALU.mult).then_inc(s_prob_ready, 1)
                    dve.wait_ge(s_probT_psum, n + 1)
                    v.tensor_copy(sprobT[:, 0:256], bank[4][:, 0:256])
                    v.tensor_copy(sprobT[0:24, 256:512], bank[4][0:24, 256:512]).then_inc(s_probT_ready, 1)
                    dve.wait_ge(s_att_psum, n + 1)
                    t0 = NP + 32 * half
                    for c in range(4):
                        ins = v.tensor_copy(mixT[:, 4 + c, t0:t0 + 32].rearrange("p (b t) -> p b t", t=ST),
                                            bank[5][:, 0:128].rearrange("p (b c t) -> p b c t", b=4, c=4)[:, :, c, :])
                    ins.then_inc(s_att_ready, 1)

                def mixed(n, chunks, r0):
                    dve.wait_ge(mixrstd_ready, n)
                    for c in chunks:
                        p = P0 + r0 + c % 4
                        v.scalar_tensor_tensor(out=mixT[:, c, :], in0=mixT[:, c, :], scalar=params[:, p:p + 1], in1=rstd_m,
                                               op0=ALU.mult, op1=ALU.mult).then_inc(mix_ready, 1)

                mixed(3 * l + 1, range(4, 8), R_ATT)
                for g in range(2):
                    dve.wait_ge(cb_psum, 2 * l + g + 1)
                    v.tensor_tensor(cbm[:, 0:NT], bank[1][:, 0:NT], upper[:, 0:NT], ALU.mult)
                    v.tensor_tensor(cbm[:, NT:UOFF[2]], bank[2][:, 0:NT - 128], upper[:, NT:UOFF[2]], ALU.mult)
                    v.tensor_tensor(cbm[0:80, UOFF[2]:UCOLS], bank[2][0:80, NT - 128:NT - 128 + 80], upper[0:80, UOFF[2]:UCOLS], ALU.mult).then_inc(cb_ready, 1)
                    dve.wait_ge(kv_stored, 32 * (l + 1))
                    if g:
                        dve.wait_ge(sstate_psum, 2 * (4 * l + 2))
                    v.tensor_tensor(Bexp[0:80, :, :], bc(Btok[0:80, 2, 128 * g:128 * g + 128], 1, SB), bc(C("batch")[0:80, :], 2, 128), ALU.mult).then_inc(Bexp_ready, 1)
                    dve.wait_ge(cb_ready, 2 * l + g + 1)
                    for pr in (2 * g, 2 * g + 1):
                        n = 4 * l + pr
                        for h in (2 * pr, 2 * pr + 1):
                            dve.wait_ge(seg_psum, 8 * l + h + 1)
                            if pr:
                                dve.wait_ge(ydiag_psum, n)
                            for j, (j0, nj) in enumerate(TILES):
                                ins = v.tensor_scalar(decay[h % 2][0:nj, UOFF[j]:UOFF[j] + NT - j0], bank[3 + h % 2][0:nj, j0:NT],
                                                      negcs[0:nj, j, h:h + 1], 0.0, ALU.add, ALU.min)
                            ins.then_inc(seg_ready, 1)
                        for half in range(2):
                            dve.wait_ge(h0T_psum, 2 * n + half + 1)
                            if pr and half == 0:
                                dve.wait_ge(yoff_psum, n)
                            v.tensor_copy(h0T_[:, 512 * half:512 * half + 512], bank[1 + half][:, :]).then_inc(h0T_ready, 1)
                        for h in (2 * pr, 2 * pr + 1):
                            dve.wait_ge(decay_exp, 8 * l + h + 1)
                            v.tensor_tensor(decay[h % 2][:, 0:UOFF[2]], decay[h % 2][:, 0:UOFF[2]], cbm[:, 0:UOFF[2]], ALU.mult)
                            v.tensor_tensor(decay[h % 2][0:80, UOFF[2]:UCOLS], decay[h % 2][0:80, UOFF[2]:UCOLS], cbm[0:80, UOFF[2]:UCOLS], ALU.mult).then_inc(M_ready, 1)
                        dve.wait_ge(wdec_ready, l + 1)
                        if pr:
                            dve.wait_ge(sstate_psum, 2 * n)
                        cols = slice(128 * pr, 128 * pr + 128)
                        for i, (t0, nn) in enumerate(TILES):
                            ins = v.tensor_tensor(xw[0:nn, i, :].rearrange("p (h d) -> p h d", h=2), xdt[0:nn, i, cols].rearrange("p (h d) -> p h d", h=2),
                                                  bc(wdec[0:nn, i, 2 * pr:2 * pr + 2], 2, 64), ALU.mult)
                        ins.then_inc(xw_ready, 1)
                        y = mixT[:, pr, :]
                        dve.wait_ge(eoff_ready, n + 1)
                        link(v.tensor_tensor(yoff, bank[7][:, 64:128], eoff, ALU.mult))
                        dve.wait_ge(ydiag_psum, n + 1)
                        v.scalar_tensor_tensor(out=y, in0=xbc[:, pr, :], scalar=dskip[l][:, pr:pr + 1], in1=bank[5 + pr % 2][:, 0:NT], op0=ALU.mult, op1=ALU.add).then_inc(y_ready, 1)
                        dve.wait_ge(y_ready, 3 * n + 1)
                        v.tensor_tensor(y[:, NP:NT], y[:, NP:NT], yoff, ALU.add).then_inc(y_ready, 1)
                        dve.wait_ge(y_ready, 3 * n + 2)
                        v.tensor_tensor(y, y, zs[:, pr, :], ALU.mult).then_inc(y_ready, 1)
                        dve.wait_ge(pstate_psum, n + 1)
                        if n:
                            dve.wait_ge(states_stored, 32 * n)
                        v.tensor_copy(pst, bank[7][:, 128:256]).then_inc(pstate_ready, 1)
                        dve.wait_ge(h0T_psum, 2 * n + 2)
                        link(v.tensor_tensor(h0, h0, bc(eoff[:, 7:64:8], 2, 128), ALU.mult))
                        for q in range(2):
                            dve.wait_ge(sstate_psum, 2 * n + q + 1)
                            v.tensor_tensor(h0_[:, 512 * q:512 * q + 512], h0_[:, 512 * q:512 * q + 512], bank[0][:, :], ALU.add).then_inc(sstate_ready, 1)
                for g in range(2):
                    mixed(3 * l + 2 + g, (2 * g, 2 * g + 1), R_SSD)
                for i in range(DK):
                    dve.wait_ge(out_psum, 8 * l + i + 1)
                    v.tensor_tensor(xT[:, i, :], xT[:, i, :], bank[3 + i % 4][:, 0:NT], ALU.add).then_inc(xT_ready, 1)
                normed(2 * l + 1, l, R_FFN, rstd_f)
                if l == 0:
                    dve.wait_ge(hn_ready, 16)
                    dve.wait_ge(states_stored, 32 * 4)
                    dve.wait_ge(outputs_stored, 16 * (2 + 2 * (3 + SB)))
                    for c in range(FC):
                        dve.wait_ge(silu_ready, c + 1)
                        dve.wait_ge(gu_psum, 2 * c + 2)
                        v.tensor_tensor(hidT[:, c, :], gate_s[c % 2], bank[3 + c % 2][:, 0:NT], ALU.mult).then_inc(hid_ready, 1)
                    for i in range(DK):
                        dve.wait_ge(down_psum, i + 1)
                        v.tensor_tensor(xT[:, i, :], xT[:, i, :], bank[(5, 6, 7, 0)[i % 4]][:, 0:NT], ALU.add).then_inc(xT_ready, 1)

            dve.wait_ge(states_stored, 32 * 4 * LAYERS)
            dve.wait_ge(outputs_stored, 16 * LAYERS * (2 + 2 * (3 + SB)))
            link(v.memset(route[:, 0:400], 0.0))
            dve.wait_ge(logit_psum, 1)
            lg, top, oh1, oh2, gate, mm_ = R(24), R(48), R(104), R(128), R(152), R(0)
            v.tensor_copy(lg[:, 0:2, :], bank[1][:, 0:16].rearrange("p (i e) -> p i e", i=2))
            link(v.tensor_copy(lg[0:80, 2, :], bank[1][0:80, 16:24]))
            for i in range(3):
                link(v.max(top[:, i, :], lg[:, i, :]))
                link(v.max_index(index8[:, 8 * i:8 * i + 8], top[:, i, :], lg[:, i, :]))
            idx = index8[:, :].rearrange("p (i e) -> p i e", i=3)
            which = R(80, 6, 2)
            link(v.tensor_copy(which, idx[:, :, 0:2]))
            iota8 = bc(iota[:, 0:8], 1, 3)
            v.tensor_tensor(oh1, iota8, which[:, :, 0:1].to_broadcast([128, 3, 8]), ALU.is_equal)
            link(v.tensor_tensor(oh2, iota8, which[:, :, 1:2].to_broadcast([128, 3, 8]), ALU.is_equal))
            v.tensor_tensor(mm_, oh1, oh2, ALU.add).then_inc(picks_counted, 1)
            ex, g1, g2 = R(96, 3, 1), R(100, 3, 1), R(88, 3, 1)
            v.tensor_tensor(ex, top[:, :, 1:2], top[:, :, 0:1], ALU.subtract).then_inc(gates_in, 1)
            dve.wait_ge(gates_exp, 1)
            link(v.tensor_scalar(g1, ex, 1.0, None, ALU.add))
            link(v.reciprocal(g1, g1))
            link(v.tensor_tensor(g2, ex, g1, ALU.mult))
            link(v.tensor_tensor(oh1, oh1, g1.to_broadcast([128, 3, 8]), ALU.mult))
            link(v.tensor_tensor(oh2, oh2, g2.to_broadcast([128, 3, 8]), ALU.mult))
            link(v.tensor_tensor(gate, oh1, oh2, ALU.add))
            dve.wait_ge(count_psum, 1)
            slot0 = R(176)
            v.tensor_copy(slot0[:, 0:2, :], bank[1][:, 32:48].rearrange("p (i e) -> p i e", i=2))
            link(v.tensor_copy(slot0[0:80, 2, :], bank[1][0:80, 48:56]))
            link(v.tensor_tensor(slot0, slot0, mm_, ALU.mult))
            link(v.tensor_scalar(slot0, slot0, -1.0, None, ALU.add))
            per = PASSES * EXPERTS + 1
            slot_of = route[:, 200:200 + 3 * per].rearrange("p (i k) -> p i k", i=3)
            gate_of = route[:, 280:280 + 3 * per].rearrange("p (i k) -> p i k", i=3)
            for b in range(PASSES):
                link(v.tensor_scalar(slot_of[:, :, EXPERTS * b:EXPERTS * b + EXPERTS], slot0, -float(SLOTS * b), None, ALU.add))
                link(v.tensor_copy(gate_of[:, :, EXPERTS * b:EXPERTS * b + EXPERTS], gate))
            link(v.tensor_reduce(route[:, 380:381], bank[1][:, 64:72], AX.X, ALU.max))
            v.tensor_copy(crowded[0:1, 0:1], route[0:1, 380:381]).then_inc(route_ready, 1)
            dve.wait_ge(route_ready, 1)
            for u in range(6):
                i, half = u // 2, u % 2
                n = TILES[i][1]
                dve.wait_ge(comb_psum, u + 1)
                v.tensor_copy(x_tok[0:n, i, 512 * half:512 * half + 512], bank[2 + u][0:n, :]).then_inc(comb_added, 1)

            def picks(k):
                if k is not first_pass:
                    dve.wait_ge(pickT_psum, k)
                for i, (t0, n) in enumerate(TILES):
                    at_slot = slot_of[0:n, i, bass.ds(k, 1)]
                    v.tensor_scalar(pick[0:n, i, :], iota[0:n, :], at_slot, None, ALU.is_equal)
                    ins = v.tensor_scalar(gpick[0:n, i, :], iota[0:n, :], at_slot, gate_of[0:n, i, bass.ds(k, 1)], ALU.is_equal, ALU.mult)
                ins.then_inc(pick_ready, 1)

            def expert_pass(k):
                dve.wait_ge(pickT_psum, k + 1)
                dve.wait_ge(comb_psum, 6 * k + 6)
                v.tensor_copy(gpickT, bank[2][:, 0:NT]).then_inc(pickT_ready, 1)
                for c in range(FC):
                    dve.wait_ge(silu_ready, k * FC + (FC + c + 1))
                    v.tensor_tensor(hid[:, c, :], gsil[c % 2], bank[3 + c % 2][:, 128:256], ALU.mult).then_inc(hid_ready, 1)
                picks(k + 1)
                for u in range(6):
                    i, half = u // 2, u % 2
                    n = TILES[i][1]
                    dve.wait_ge(comb_psum, 6 * k + (u + 7))
                    part = x_tok[0:n, i, 512 * half:512 * half + 512]
                    dve.wait_ge(comb_added, 6 * k + 6)
                    v.tensor_tensor(part, part, bank[5 + u % 3][0:n, :], ALU.add).then_inc(comb_added, 1)

            picks(first_pass)
            with dve.Fori(0, EXPERTS) as e:
                expert_pass(e)
            fullest = dve.value_load(crowded[0:1, 0:1], min_val=0, max_val=NT)
            dve.wait_ge(comb_added, 6 * EXPERTS + 6)
            with dve.If(fullest > SLOTS):
                with dve.Fori(1, PASSES) as b:
                    with dve.Fori(0, EXPERTS) as e:
                        expert_pass(b * EXPERTS + e)
                dve.wait_ge(comb_added, 6 * EXPERTS * PASSES + 6)
            v.memset(route[:, 390:391], 0.0).then_inc(all_added, 1)


def tail_view(raw, k):
    return raw[:, k, NP:RAWC].rearrange("p (j r) -> p j r", r=ST + 3)[:, :, 0:3]


def samples_of_conv(conv, k):
    return conv[:, k, S0:NPAD].rearrange("p (b t) -> p b t", t=ST + 3)[:, :, 0:ST]


_INS = ["x_prompt", "x_sample", "state_ssm", "state_conv", "cache_meta_k", "cache_meta_v", "cache_win_k", "cache_win_v",
        "meta_tokens", "norm_mix_w", "w_in", "conv_w", "conv_b", "dt_bias", "a_log", "d_skip", "ssd_norm_w", "q_norm_w",
        "k_norm_w", "sinks", "attn_norm_w", "w_out", "norm_ffn_w", "w_gate", "w_up", "w_down", "w_router", "moe_w_gate",
        "moe_w_up", "moe_w_down"]
_KV = (64,)
_OUTS = [("y_prompt", (1, 256, 1024)), ("y_sample", (8, 8, 1024)), ("p_ssm", (2, 1, 8, 64, 128)), ("p_conv", (2, 1, 3, 1024)),
         ("p_meta_k", (2, 1, 16, 2, 64)), ("p_meta_v", (2, 1, 16, 2, 64)), ("p_win_k", (2, 1, 128, 2, 64)), ("p_win_v", (2, 1, 128, 2, 64)),
         ("s_ssm", (2, 8, 8, 64, 128)), ("s_conv", (2, 8, 3, 1024)), ("s_win_k", (2, 8, 128, 2, 64)), ("s_win_v", (2, 8, 128, 2, 64))]


def kernel(**inputs):
    import numpy as _np
    import concourse.bacc as _bacc
    from concourse.bass_utils import run_bass_kernel_spmd as _run

    nc = _bacc.Bacc("TRN2", target_bir_lowering=False, num_devices=1)
    arrays, ins, outs = {}, {}, {}
    for name in _INS:
        x = _np.ascontiguousarray(inputs[name])
        arrays[f"in_{name}"] = x
        ins[name] = nc.dram_tensor(f"in_{name}", x.shape, F32, kind="ExternalInput").ap()
    arrays["in_const"] = CONST
    ins["const"] = nc.dram_tensor("in_const", CONST.shape, F32, kind="ExternalInput").ap()
    for name, shape in _OUTS:
        outs[name] = nc.dram_tensor(f"out_{name}", shape, F32, kind="ExternalOutput").ap()
    hymba_step(nc, ins, outs)
    r = _run(nc, [arrays], core_ids=[0])
    return tuple(r.results[0][f"out_{name}"] for name, _ in _OUTS)
```

```python
from contextlib import ExitStack

import numpy as np

import concourse.bass as bass
from concourse import mybir

F32 = mybir.dt.float32
U32 = mybir.dt.uint32
I32 = mybir.dt.int32
ALU = mybir.AluOpType
ACT = mybir.ActivationFunctionType
AX = mybir.AxisListType

D = 1024
DK = D // 128
LAYERS = 2
META, SEQ = 16, 256
NP = META + SEQ
SB, ST = 8, 8
NT = NP + SB * ST
TILES = ((0, 128), (128, 128), (256, NT - 256))
HEADS, STATE, CONV_W = 8, 128, 4
NPAD = NP + 3 + SB * (ST + 3)
RAWC = NP + (SB + 1) * (ST + 3)
NCONV = NPAD - 3
S0 = NP + 3
WIN = 128
FF = 2816
FC = FF // 128
EXPERTS = 8
SLOTS = 112
PASSES = -(-NT // SLOTS)
EPS = 1e-6
NEG = -1e30
PAST = 2048
RING, SLAB = 11, 2048
GU_SLABS = FC
DOWN_SLABS = FC // 2
FFN_SLABS = GU_SLABS + DOWN_SLABS
IN_SLABS, OUT_SLABS = 9, 4

UPPER = ((0, NT), (128, NT), (256, NT))
UOFF = (0, NT, NT + NT - 128)
UCOLS = NT + (NT - 128) + (NT - 256)
LOWER = (128, 256, NT)
LOFF = (0, 128, 384)
LCOLS = 128 + 256 + NT

PARAM_ROWS = 64
R_MIX, R_FFN, R_CW, R_CB, R_SSD, R_ATT = 0, 8, 16, 48, 56, 60


def constants():
    t = np.arange(NT)
    seq = np.where(t < NP, 0, 1 + (t - NP) // ST)
    same = seq[:, None] == seq[None, :]
    upper = (same & (t[:, None] <= t[None, :])).astype(np.float32)
    lower = (same & (t[:, None] > t[None, :])).astype(np.float32)

    def rows(a):
        return np.pad(a, ((0, 128 - a.shape[0]), (0, 0)))

    parts = {"ident": np.eye(128, dtype=np.float32)}
    parts["upper"] = np.concatenate([rows(upper[a:a + n, UPPER[i][0]:]) for i, (a, n) in enumerate(TILES)], 1)
    parts["lower"] = np.concatenate([rows(lower[a:a + n, :LOWER[i]]) for i, (a, n) in enumerate(TILES)], 1)
    parts["halves"] = np.kron(np.eye(2), np.ones((64, 64))).astype(np.float32)
    turn = np.zeros((128, 128), np.float32)
    for m in range(128):
        if m % 64 < 32:
            turn[m + 32, m] = -1.0
        else:
            turn[m - 32, m] = 1.0
    parts["turn"] = turn
    pos = np.where(t < NP, t, PAST + (t - NP) % ST).astype(np.float32)
    inv = np.float32(10000.0) ** (-np.arange(32, dtype=np.float32) / np.float32(32))
    ang = (pos[None, :] * inv[np.arange(128) % 32][:, None]).astype(np.float32).astype(np.float64)
    parts["cos"] = np.cos(ang).astype(np.float32)
    parts["sin"] = np.sin(ang).astype(np.float32)

    def mask(ok):
        return rows(np.where(ok, 0.0, NEG).astype(np.float32))

    def prompt(i0, ni, nj):
        i, j = np.arange(i0, i0 + ni)[:, None], np.arange(nj)[None, :]
        return mask((j <= i) & ((j < META) | (i - j < WIN)))

    parts["mask0"] = prompt(0, 128, 128)
    parts["mask1"] = prompt(128, 128, 256)
    parts["mask2"] = prompt(256, NP - 256, NP)
    tq = (np.arange(128) % ST)[:, None]
    w, n = np.arange(WIN)[None, :], np.arange(ST)[None, :]
    parts["mask_s"] = mask(np.concatenate([w > tq, np.ones((128, META), bool), n <= tq], 1))
    parts["batch"] = rows(np.concatenate([np.zeros((NP - 256, SB)), np.kron(np.eye(SB), np.ones((ST, 1)))]).astype(np.float32))
    parts["iota"] = np.tile(np.arange(128, dtype=np.float32), (128, 1))
    at, n = {}, 0
    for name, a in parts.items():
        at[name] = (n, a.shape[1])
        n += a.shape[1]
    return np.ascontiguousarray(np.concatenate(list(parts.values()), 1), dtype=np.float32), at


CONST, CONST_AT = constants()


def bc(ap, axis, n):
    a = ap.unsqueeze(axis)
    shape = list(a.shape)
    shape[axis] = n
    return a.to_broadcast(shape)


def weight_loads(a, l):
    whole = slice(0, 128)

    def cols(w, c0, n=256):
        return [(whole, lambda s: s.rearrange("p (k n) -> p k n", k=DK), w[:, c0:c0 + n].rearrange("(k p) n -> p k n", p=128))]

    w = a["w_in"][l]
    slabs = [cols(w, 2056)]
    for half in range(2):
        loads = []
        for cc in range(2):
            for g in range(2):
                c0 = 1544 + g * 256 + (2 * half + cc) * 64
                loads.append((whole, lambda s, o=cc * 128 + g * 64: s.rearrange("p (k n) -> p k n", k=DK)[:, :, o:o + 64],
                              w[:, c0:c0 + 64].rearrange("(k p) n -> p k n", p=128)))
        slabs.append(loads)
    slabs += [cols(w, 512 + 256 * i) for i in range(4)]
    slabs += [cols(w, 256 * i) for i in range(2)]
    w = a["w_out"][l]
    for i in range(OUT_SLABS):
        c0 = 256 * i
        loads = [(whole, lambda s: s.rearrange("p (k n) -> p k n", k=DK)[:, 0:4, :],
                  w[0:512, c0:c0 + 256].rearrange("(k p) n -> p k n", p=128))]
        for g in range(2):
            loads.append((slice(64 * g, 64 * g + 64), lambda s: s.rearrange("p (k n) -> p k n", k=DK)[:, 4:8, :],
                          w[512 + 256 * g:768 + 256 * g, c0:c0 + 256].rearrange("(c d) n -> d c n", d=64)))
        slabs.append(loads)
    if l == 0:
        for u in range(FC // 2):
            slabs.append(cols(a["w_gate"][0], 256 * u))
            slabs.append(cols(a["w_up"][0], 256 * u))
        blocks = [(half, f) for half in range(2) for f in range(FC)]
        for i in range(DOWN_SLABS):
            loads = []
            for half in range(2):
                mine = [(j, f) for j, (h, f) in enumerate(blocks[4 * i:4 * i + 4]) if h == half]
                if mine:
                    j0, f0, n = mine[0][0], mine[0][1], len(mine)
                    loads.append((whole, lambda s, j0=j0, n=n: s.rearrange("p (j n) -> p j n", j=4)[:, j0:j0 + n, :],
                                  a["w_down"][0][f0 * 128:(f0 + n) * 128, 512 * half:512 * half + 512]
                                  .rearrange("(j p) n -> p j n", p=128)))
            slabs.append(loads)
    return slabs


def hymba_step(nc, a, o):
    fixed = weight_loads(a, 0) + weight_loads(a, 1)
    seen = [0] * RING
    arrives = []
    for n, loads in enumerate(fixed):
        seen[n % RING] += 16 * len(loads)
        arrives.append(seen[n % RING])
    fixed_seen = list(seen)
    FIRST = (0, IN_SLABS + OUT_SLABS + FFN_SLABS)
    MOE0 = len(fixed)
    scope = ExitStack()
    with scope:
        def sb(name, cols, dt=F32, rows=128):
            return scope.enter_context(nc.sbuf_tensor(name, [rows, cols], dt))

        def sem(name):
            return scope.enter_context(nc.semaphore(name))

        bank = [scope.enter_context(nc.psum_tensor(f"bank{i}", [128, 512], F32)) for i in range(8)]
        const = sb("const", CONST.shape[1])
        ring = sb("ring", RING * SLAB)
        xT_ = sb("xT", DK * NT)
        hnT_ = sb("hnT", DK * NT)
        params = sb("params", 128)
        small = sb("small", 512)
        arena_cols = 20900
        arena = sb("arena", arena_cols)
        index8 = sb("index8", 24, U32)
        crowded = sb("crowded", 1, I32)

        def C(name):
            at, n = CONST_AT[name]
            return const[:, at:at + n]

        ident, halves, turn, cosT, sinT, iota = (C(x) for x in ("ident", "halves", "turn", "cos", "sin", "iota"))
        upper, lower = C("upper"), C("lower")
        xT = xT_[:, :].rearrange("p (k t) -> p k t", k=DK)
        hnT = hnT_[:, :].rearrange("p (k t) -> p k t", k=DK)
        mixT = hnT
        slots = [ring[:, i * SLAB:(i + 1) * SLAB] for i in range(RING)]

        at = [0]

        def take(n):
            at[0] += n
            assert at[0] <= arena_cols, at[0]
            return arena[:, at[0] - n:at[0]]

        qk_ = take(5 * NT)
        qk = qk_.rearrange("p (k t) -> p k t", k=5)
        zs = take(4 * NT).rearrange("p (k t) -> p k t", k=4)
        raw_ = take(DK * RAWC)
        raw = raw_.rearrange("p (k t) -> p k t", k=DK)
        xbc = raw_[:, 0:DK * NT].rearrange("p (k t) -> p k t", k=DK)
        conv_ = take(DK * NPAD)
        conv = conv_.rearrange("p (k t) -> p k t", k=DK)
        probs_of = [conv_[:, i * 656:(i + 1) * 656] for i in range(3)]
        probsT_of = [conv_[:, 1968 + i * 432:2400 + i * 432] for i in range(2)]
        xdt = take(3 * 512).rearrange("p (i n) -> p i n", i=3)
        Btok = take(3 * 256).rearrange("p (i n) -> p i n", i=3)
        ktok = take(3 * 128).rearrange("p (i n) -> p i n", i=3)
        vtok = take(3 * 128).rearrange("p (i n) -> p i n", i=3)
        h0_ = [take(1024), conv_[:, 1880:2904]]
        h0 = [x.rearrange("p (b n) -> p b n", b=SB) for x in h0_]
        h0T_ = take(1024)
        h0T = h0T_.rearrange("p (b n) -> p b n", b=SB)
        tmp2 = [arena[:, at[0] - 2048 + 1008 * i:at[0] - 2048 + 1008 * (i + 1)].rearrange("p (j t) -> p j t", j=3)
                for i in range(2)]
        Bexp_ = take(1024)
        Bexp = Bexp_.rearrange("p (b n) -> p b n", b=SB)
        tails = Bexp_
        decay = [take(UCOLS) for _ in range(2)] + [qk_[:, i * UCOLS:(i + 1) * UCOLS] for i in range(2)]
        cbm = take(UCOLS)
        tail_cols = decay[0][:, 0:27 * DK].rearrange("p (k n) -> p k n", k=DK)
        qs = decay[1][:, 0:256].rearrange("p (b c t) -> p b c t", b=SB, c=4)
        xw = take(384).rearrange("p (i n) -> p i n", i=3)
        pst = [take(128) for _ in range(2)]
        yoff = take(64)
        eoff = take(64)
        winK = take(512).rearrange("p (b n) -> p b n", b=4)
        winV = take(512).rearrange("p (b n) -> p b n", b=4)
        mnV = take(512).rearrange("p (b n) -> p b n", b=4)
        winKT = cbm[:, 0:512]
        metK = take(128)
        metKT = cbm[:, 512:576]
        sprob_ = take(304)
        sprob = sprob_.rearrange("p (g n) -> p g n", g=2)
        sprobT = take(512)
        rstd = take(NT)
        rstd_m = take(NT)
        wdt = take(64).rearrange("p (k n) -> p k n", k=DK)
        xtok_in = arena[:, 9 * NT:9 * NT + 3 * D]
        xtok_in = xtok_in.rearrange("p (i n) -> p i n", i=3)
        squares = [arena[:, at9:at9 + DK * NT].rearrange("p (k t) -> p k t", k=DK) for at9 in (9 * NT + DK * RAWC + DK * NPAD, 9 * NT + DK * RAWC)]
        hidT = arena[:, 0:FC * NT].rearrange("p (f t) -> p f t", f=FC)
        gate_s = [arena[:, FC * NT + i * NT:FC * NT + (i + 1) * NT] for i in range(2)]
        rstd_f = rstd_m
        hn_tok = arena[:, 0:3072].rearrange("p (i n) -> p i n", i=3)
        x_tok = arena[:, 3072:6144].rearrange("p (i n) -> p i n", i=3)
        hid = arena[:, 6144:6144 + FC * SLOTS].rearrange("p (f s) -> p f s", f=FC)
        xg_ = arena[:, 9000:9000 + DK * SLOTS]
        xg = xg_.rearrange("p (k s) -> p k s", k=DK)
        ytok = arena[0:SLOTS, 10100:11124]
        pick = arena[:, 11200:11200 + 3 * SLOTS].rearrange("p (i s) -> p i s", i=3)
        gpick = arena[:, 11600:11600 + 3 * SLOTS].rearrange("p (i s) -> p i s", i=3)
        gpickT = arena[0:SLOTS, 12000:12000 + NT]
        gsil = [arena[:, 12400 + 128 * i:12400 + 128 * i + SLOTS] for i in range(2)]
        route = arena[:, 12700:13100]
        wr = arena[:, 13200:13264].rearrange("p (k n) -> p k n", k=DK)

        def R(i, n=24, w=8):
            return route[:, i:i + n].rearrange("p (i e) -> p i e", e=w)

        sm = [0]

        def little(n):
            sm[0] += n
            assert sm[0] <= 512
            return small[:, sm[0] - n:sm[0]]

        eps = little(1)
        qkw = [little(1) for _ in range(4)]
        dskip = [little(4) for _ in range(LAYERS)]
        sinks = [little(8) for _ in range(LAYERS)]
        sink_s = [little(2) for _ in range(LAYERS)]
        dtb = [little(8) for _ in range(LAYERS)]
        alog = [little(8) for _ in range(LAYERS)]
        nega = little(8)
        dt = little(24).rearrange("p (i h) -> p i h", i=3)
        dta = little(24).rearrange("p (i h) -> p i h", i=3)
        dw = [little(24) for _ in range(5)]
        negcs = little(24).rearrange("p (i h) -> p i h", i=3)
        wdec = little(24).rearrange("p (i h) -> p i h", i=3)
        mx = [little(3) for _ in range(3)]
        nm = [little(3) for _ in range(3)]
        sums = [little(3) for _ in range(3)]
        es = [little(3) for _ in range(3)]
        csrow = rstd[0:8, :]
        ones = sb("ones", 128)

        slab_here = [sem(f"slab_here{i}") for i in range(RING)]
        slab_free = sem("slab_free")
        const_here, tokens_here, params_here, small_here, sinks_here = (
            sem(x) for x in ("const_here", "tokens_here", "params_here", "small_here", "sinks_here"))
        dtw_here, conv_rows_here, caches_here, router_here = sem("dtw_here"), sem("conv_rows_here"), sem("caches_here"), sem("router_here")
        mnv_new_here, h0_here = sem("mnv_new_here"), [sem(f"h0_here{i}") for i in range(2)]
        states_stored, kv_stored, outputs_stored = [sem(f"states_stored{i}") for i in range(2)], sem("kv_stored"), sem("outputs_stored")
        set_up, params_psum, params_ready = sem("set_up"), sem("params_psum"), sem("params_ready")
        xin_psum, xT_ready = sem("xin_psum"), sem("xT_ready")
        squares_ready, sum_psum, rstd_ready, hn_ready = sem("squares_ready"), sem("sum_psum"), sem("rstd_ready"), sem("hn_ready")
        prev_psum, prev_ready = sem("prev_psum"), sem("prev_ready")
        proj_psum, proj_dve, proj_raw, proj_z = sem("proj_psum"), sem("proj_dve"), sem("proj_raw"), sem("proj_z")
        qksq_ready, qksum_psum, qkrstd_ready, qkn_ready, rot_psum, qk_ready = (
            sem(x) for x in ("qksq_ready", "qksum_psum", "qkrstd_ready", "qkn_ready", "rot_psum", "qk_ready"))
        conv_ready, xbc_ready, tail_psum, tail_ready = sem("conv_ready"), sem("xbc_ready"), sem("tail_psum"), sem("tail_ready")
        dt_exp_in, dt_exp, dt_ln_in, dt_ln, dta_ready, cs_psum, cs_ready, wdec_ready = (
            sem(x) for x in ("dt_exp_in", "dt_exp", "dt_ln_in", "dt_ln", "dta_ready", "cs_psum", "cs_ready", "wdec_ready"))
        tok_psum, tok_ready = sem("tok_psum"), sem("tok_ready")
        tail_cols_ready, qs_ready = sem("tail_cols_ready"), sem("qs_ready")
        score_psum, negmax_ready, exp_ready, prob_ready, probT_psum, probT_ready, att_psum, att_ready = (
            sem(x) for x in ("score_psum", "negmax_ready", "exp_ready", "prob_ready", "probT_psum", "probT_ready", "att_psum", "att_ready"))
        s_KT_psum, s_KT_ready, s_score_psum, s_negmax_ready, s_exp_ready, s_prob_ready, s_probT_psum, s_probT_ready, s_att_psum, s_att_ready = (
            sem(x) for x in ("s_KT_psum", "s_KT_ready", "s_score_psum", "s_negmax_ready", "s_exp_ready", "s_prob_ready",
                             "s_probT_psum", "s_probT_ready", "s_att_psum", "s_att_ready"))
        cb_psum, cb_ready, seg_psum, seg_ready, decay_exp, M_ready, ydiag_psum, yoff_psum, eoff_ready, y_ready = (
            sem(x) for x in ("cb_psum", "cb_ready", "seg_psum", "seg_ready", "decay_exp", "M_ready", "ydiag_psum", "yoff_psum", "eoff_ready", "y_ready"))
        Bexp_ready, h0T_psum, h0T_ready, xw_ready, pstate_psum, pstate_ready, sstate_psum, sstate_ready = (
            sem(x) for x in ("Bexp_ready", "h0T_psum", "h0T_ready", "xw_ready", "pstate_psum", "pstate_ready", "sstate_psum", "sstate_ready"))
        mixsq_ready, mixsum_psum, mixrstd_ready, mix_ready, out_psum = (
            sem(x) for x in ("mixsq_ready", "mixsum_psum", "mixrstd_ready", "mix_ready", "out_psum"))
        gu_psum, silu_ready, hid_ready, down_psum = sem("gu_psum"), sem("silu_ready"), sem("hid_ready"), sem("down_psum")
        logit_psum, gates_in, gates_exp, picks_counted, count_psum, route_ready = (
            sem(x) for x in ("logit_psum", "gates_in", "gates_exp", "picks_counted", "count_psum", "route_ready"))
        turn_psum, turn_act = sem("turn_psum"), sem("turn_act")
        pick_ready, xg_psum, xg_ready, pickT_psum, pickT_ready = (sem(x) for x in ("pick_ready", "xg_psum", "xg_ready", "pickT_psum", "pickT_ready"))
        y_psum, ytok_ready, comb_psum, comb_added, all_added = (sem(x) for x in ("y_psum", "ytok_ready", "comb_psum", "comb_added", "all_added"))
        dve_step, act_step = sem("dve_step"), sem("act_step")

        block = scope.enter_context(nc.Block())
        first_pass = 0

        def slab(n):
            return slots[n % RING]

        def wait_slab(pe, n):
            pe.wait_ge(slab_here[n % RING], arrives[n])

        @block.sync
        def _(sp):
            xp, xs, mt = a["x_prompt"][0], a["x_sample"].rearrange("b t d -> (b t) d"), a["meta_tokens"]
            sp.dma_start(xtok_in[0:META, 0, :], mt).then_inc(tokens_here, 16)
            sp.dma_start(xtok_in[META:128, 0, :], xp[0:112, :]).then_inc(tokens_here, 16)
            sp.dma_start(xtok_in[:, 1, :], xp[112:240, :]).then_inc(tokens_here, 16)
            sp.dma_start(xtok_in[0:16, 2, :], xp[240:256, :]).then_inc(tokens_here, 16)
            sp.dma_start(xtok_in[16:80, 2, :], xs).then_inc(tokens_here, 16)
            sp.dma_start(const[:, :], a["const"]).then_inc(const_here, 16)
            for n, loads in enumerate(fixed):
                if n >= RING:
                    sp.wait_ge(slab_free, n - RING + 1)
                for rows, view, src in loads:
                    sp.dma_start(view(slab(n)[rows, :]), src).then_inc(slab_here[n % RING], 16)

            def expert_slabs(k, e):
                for j in range(FFN_SLABS):
                    s = (MOE0 + j) % RING
                    sp.wait_ge(slab_free, k * FFN_SLABS + (MOE0 + j - RING + 1))
                    if j < GU_SLABS:
                        w = a["moe_w_gate"] if j % 2 == 0 else a["moe_w_up"]
                        c0 = 256 * (j // 2)
                        dst = slots[s].rearrange("p (k n) -> p k n", k=DK)
                        src = w[0, e, :, c0:c0 + 256].rearrange("(k p) n -> p k n", p=128)
                    else:
                        r0 = 256 * (j - GU_SLABS)
                        dst = slots[s].rearrange("p (r n) -> p r n", r=2)
                        src = a["moe_w_down"][0, e, r0:r0 + 256, :].rearrange("(r p) n -> p r n", p=128)
                    sp.dma_start(dst, src).then_inc(slab_here[s], 16)

            with sp.Fori(0, EXPERTS) as e:
                expert_slabs(e, e)
            sp.wait_ge(route_ready, 1)
            fullest = sp.value_load(crowded[0:1, 0:1], min_val=0, max_val=NT)
            with sp.If(fullest > SLOTS):
                with sp.Fori(1, PASSES) as b:
                    with sp.Fori(0, EXPERTS) as e:
                        expert_slabs(b * EXPERTS + e, e)

        @block.gpsimd
        def _(pool):
            pool.memset(ones[:, :], 1.0).then_inc(set_up, 1)
            pool.memset(small[:, :], 0.0).then_inc(set_up, 1)
            pool.wait_ge(set_up, 2)
            pool.memset(eps, EPS).then_inc(set_up, 1)
            with nc.allow_non_contiguous_dma(reason="small tables"):
                def sample_caches(l, half):
                    bs = slice(4 * half, 4 * half + 4)
                    pool.dma_start(winK, a["cache_win_k"][l, bs].rearrange("b w g d -> w b (g d)")).then_inc(caches_here, 16)
                    pool.dma_start(winV, a["cache_win_v"][l, bs].rearrange("b w g d -> w b (g d)")).then_inc(caches_here, 16)
                    pool.dma_start(metK[0:64, :], a["cache_meta_k"][l, bs].rearrange("b w g d -> (b w) (g d)")).then_inc(caches_here, 16)
                    pool.dma_start(mnV[0:META, :, :], a["cache_meta_v"][l, bs].rearrange("b w g d -> w b (g d)")).then_inc(caches_here, 16)

                def new_values(half):
                    for b in range(4):
                        r0 = 16 + 8 * (4 * half + b)
                        pool.dma_start(mnV[META:META + ST, b, :], vtok[r0:r0 + ST, 2, :]).then_inc(mnv_new_here, 16)

                def load_wdt(l):
                    pool.dma_start(wdt, a["w_in"][l][:, 1536:1544].rearrange("(k p) n -> p k n", p=128)).then_inc(dtw_here, 16)

                def load_conv_rows(l):
                    pool.dma_start(tails[0:24, :], a["state_conv"][l].rearrange("b r n -> (b r) n")).then_inc(conv_rows_here, 16)

                load_conv_rows(0)
                load_wdt(0)
                pool.wait_ge(set_up, 3)
                for l in range(LAYERS):
                    for g in range(2):
                        half = slice(64 * g, 64 * g + 64)
                        pool.dma_start(qkw[2 * l][half, :], a["k_norm_w"][l].rearrange("(d o) -> d o", o=1)).then_inc(small_here, 16)
                        pool.dma_start(qkw[2 * l + 1][half, :], a["q_norm_w"][l].rearrange("(d o) -> d o", o=1)).then_inc(small_here, 16)
                        pool.dma_start(dskip[l][half, :], a["d_skip"][l][g:8:2].partition_broadcast(64)).then_inc(small_here, 16)
                    pool.dma_start(sinks[l], a["sinks"][l].partition_broadcast(128)).then_inc(small_here, 16)
                    pool.dma_start(dtb[l], a["dt_bias"][l].partition_broadcast(128)).then_inc(small_here, 16)
                    pool.dma_start(alog[l], a["a_log"][l].partition_broadcast(128)).then_inc(small_here, 16)
                for l in range(LAYERS):
                    if l:
                        pool.wait_ge(xT_ready, 24)
                        load_wdt(l)
                        load_conv_rows(l)
                    sample_caches(l, 0)
                    for kind, src, dst in (("k", a["cache_win_k"], o["s_win_k"]), ("v", a["cache_win_v"], o["s_win_v"])):
                        pool.dma_start(dst[l, :, 0:WIN - ST].rearrange("b w g d -> b w (g d)"),
                                       src[l, :, ST:WIN].rearrange("b w g d -> b w (g d)")).then_inc(outputs_stored, 16)
                    for r in range(16):
                        pool.dma_start(sink_s[l][8 * r:8 * r + 8, :],
                                       a["sinks"][l][r % 4:8:4].partition_broadcast(8)).then_inc(sinks_here, 16)
                    pool.wait_ge(tail_ready, 2 * (l + 1))
                    pool.dma_start(o["p_conv"][l, 0], tails[0:3, :]).then_inc(kv_stored, 16)
                    pool.dma_start(o["s_conv"][l].rearrange("b r n -> (b r) n"), tails[3:27, :]).then_inc(kv_stored, 16)
                    pool.wait_ge(tok_ready, 8 * (l + 1))
                    pool.wait_ge(proj_dve, 7 * l + 1)
                    new_values(0)
                    for name, t in (("k", ktok), ("v", vtok)):
                        def rows(ap):
                            return ap.rearrange("w g d -> w (g d)")
                        pool.dma_start(rows(o[f"p_meta_{name}"][l, 0]), t[0:META, 0, :]).then_inc(outputs_stored, 16)
                        pool.dma_start(rows(o[f"p_win_{name}"][l, 0, 0:112]), t[16:128, 1, :]).then_inc(outputs_stored, 16)
                        pool.dma_start(rows(o[f"p_win_{name}"][l, 0, 112:128]), t[0:16, 2, :]).then_inc(outputs_stored, 16)
                        for b in range(SB):
                            pool.dma_start(rows(o[f"s_win_{name}"][l, b, WIN - ST:WIN]), t[16 + 8 * b:24 + 8 * b, 2, :]).then_inc(outputs_stored, 16)
                    pool.wait_ge(s_att_psum, 2 * l + 1)
                    pool.wait_ge(mnv_new_here, 16 * (8 * l + 4))
                    sample_caches(l, 1)
                    new_values(1)
                    def load_states(pr):
                        n = 4 * l + pr
                        pool.dma_start(h0[n % 2], a["state_ssm"][l, :, 2 * pr:2 * pr + 2].rearrange("b h p n -> (h p) b n")).then_inc(h0_here[n % 2], 16)

                    pool.wait_ge(qk_ready, 5 * (l + 1))
                    load_states(0)
                    pool.wait_ge(att_psum, 4 * (l + 1))
                    load_states(1)
                    for pr in range(4):
                        n = 4 * l + pr
                        pool.wait_ge(pstate_ready, n + 1)
                        pool.dma_start(o["p_ssm"][l, 0, 2 * pr:2 * pr + 2].rearrange("h p n -> (h p) n"), pst[n % 2]).then_inc(states_stored[n % 2], 16)
                        pool.wait_ge(sstate_ready, 2 * (n + 1))
                        pool.dma_start(o["s_ssm"][l, :, 2 * pr:2 * pr + 2].rearrange("b h p n -> (h p) b n"), h0[n % 2]).then_inc(states_stored[n % 2], 16)
                        if pr < 2:
                            pool.wait_ge(states_stored[n % 2], 32 * (n // 2 + 1))
                            load_states(pr + 2)
                pool.wait_ge(xT_ready, 32)
                pool.dma_start(wr, a["w_router"][0].rearrange("(k p) n -> p k n", p=128)).then_inc(router_here, 16)
                pool.wait_ge(all_added, 1)
                yp, ys = o["y_prompt"][0], o["y_sample"].rearrange("b t d -> (b t) d")
                pool.dma_start(yp[0:112, :], x_tok[META:128, 0, :]).then_inc(outputs_stored, 16)
                pool.dma_start(yp[112:240, :], x_tok[:, 1, :]).then_inc(outputs_stored, 16)
                pool.dma_start(yp[240:256, :], x_tok[0:16, 2, :]).then_inc(outputs_stored, 16)
                pool.dma_start(ys, x_tok[16:80, 2, :]).then_inc(outputs_stored, 16)
            pool.wait_ge(outputs_stored, 16 * (LAYERS * (2 + 2 * (3 + SB)) + 4))
            pool.wait_ge(kv_stored, 32 * LAYERS)
            for i in range(2):
                pool.wait_ge(states_stored[i], 64 * LAYERS)

        @block.tensor
        def _(pe):
            mm = nc.tensor.matmul
            owed = [0]

            def pay(ins):
                if owed[0]:
                    ins.then_inc(slab_free, 1)
                    owed[0] -= 1
                return ins

            def norm_sums(n):
                for k in range(DK):
                    pe.wait_ge(squares_ready, DK * n + k + 1)
                    i = mm(bank[0][:, 0:NT], ones[:, :], squares[n % 2][:, k, :], start=(k == 0), stop=(k == DK - 1))
                    if k < DK - 1:
                        pay(i)
                i.then_inc(sum_psum, 1)

            pe.wait_ge(const_here, 16)
            pe.wait_ge(set_up, 3)
            pe.wait_ge(tokens_here, 80)
            for k in range(DK):
                if k >= 4:
                    pe.wait_ge(xT_ready, k - 3)
                for i, (t0, n) in enumerate(TILES):
                    ins = nc.tensor.transpose(bank[1 + k % 4][:, t0:t0 + n], xtok_in[0:n, i, 128 * k:128 * k + 128], ident[0:n, 0:n])
                ins.then_inc(xin_psum, 1)
            pe.wait_ge(params_here, 16 * 7 * LAYERS)
            nc.tensor.transpose(bank[7][:, 0:128], conv_[:, 128:256], ident).then_inc(params_psum, 1)

            for l in range(LAYERS):
                s0 = FIRST[l]
                norm_sums(2 * l)
                pe.wait_ge(conv_rows_here, 16 * (l + 1))
                pe.wait_ge(xT_ready, 8 if l == 0 else 24)
                for k in range(DK):
                    ins = nc.tensor.transpose(bank[1][:, 24 * k:24 * k + 24], tails[0:24, 128 * k:128 * k + 128], ident[0:24, 0:24])
                ins.then_inc(prev_psum, 1)
                pe.wait_ge(prev_ready, l + 1)
                pe.wait_ge(dtw_here, 16 * (l + 1))

                def column_chunk(out, w, c0):
                    for k in range(DK):
                        ins = mm(out, w[:, k, c0:c0 + 128], hnT[:, k, :], start=(k == 0), stop=(k == DK - 1))
                        if k < DK - 1:
                            pay(ins)
                    return ins

                def sl(n):
                    return slab(s0 + n).rearrange("p (k n) -> p k n", k=DK)

                wait_slab(pe, s0)
                for i, (t0, n) in enumerate(TILES):
                    for k in range(DK):
                        if i == 0:
                            pe.wait_ge(hn_ready, 8 * 2 * l + k + 1)
                        mm(bank[1][0:n, 128 * i:128 * i + 128], hnT[:, k, t0:t0 + n], sl(0)[:, k, 128:256], start=(k == 0), stop=(k == DK - 1))
                for i, (t0, n) in enumerate(TILES):
                    for k in range(DK):
                        ins = mm(bank[1][0:n, 384 + 8 * i:392 + 8 * i], hnT[:, k, t0:t0 + n], wdt[:, k, :], start=(k == 0), stop=(k == DK - 1))
                ins.then_inc(proj_psum, 1)
                column_chunk(bank[2][:, 0:NT], sl(0), 0).then_inc(proj_psum, 1)
                owed[0] += 1
                for c in range(4):
                    wait_slab(pe, s0 + 1 + c // 2)
                    if c >= 2:
                        pe.wait_ge(proj_dve, 7 * l + (2 if c == 2 else 3))
                    column_chunk(bank[1 + (2 + c) % 4][:, 0:NT], sl(1 + c // 2), 128 * (c % 2)).then_inc(proj_psum, 1)
                    owed[0] += c % 2
                for step in range(8):
                    wait_slab(pe, s0 + 3 + step // 2)
                    n = 6 + step
                    if step < 4:
                        pe.wait_ge(proj_dve, 7 * l + 4 + step)
                    else:
                        pe.wait_ge(proj_raw, 8 * l + step - 3)
                    column_chunk(bank[1 + n % 4][:, 0:NT], sl(3 + step // 2), 128 * (step % 2)).then_inc(proj_psum, 1)
                    owed[0] += step % 2
                    if step < 5:
                        pe.wait_ge(qksq_ready, 5 * l + step + 1)
                        if step >= 2:
                            pe.wait_ge(qkrstd_ready, 5 * l + step - 1)
                        mm(bank[5 + step % 2][:, 0:NT], halves, tmp2[step % 2][:, 0, :], start=True, stop=True).then_inc(qksum_psum, 1)
                    if 1 <= step <= 5:
                        pe.wait_ge(qkn_ready, 5 * l + step)
                        if step >= 3:
                            pe.wait_ge(qk_ready, 5 * l + step - 2)
                        else:
                            pe.wait_ge(rstd_ready, 2 * l + 1)
                        mm(bank[(7, 0)[(step - 1) % 2]][:, 0:NT], turn, qk[:, step - 1, :], start=True, stop=True).then_inc(rot_psum, 1)
                for c in range(4):
                    wait_slab(pe, s0 + 7 + c // 2)
                    n = 14 + c
                    pe.wait_ge(proj_raw, 8 * l + 5 + c)
                    column_chunk(bank[1 + n % 4][:, 0:NT], sl(7 + c // 2), 128 * (c % 2)).then_inc(proj_psum, 1)
                    owed[0] += c % 2
                pe.wait_ge(qkrstd_ready, 5 * (l + 1))
                pe.wait_ge(tail_cols_ready, l + 1)
                for k in range(DK):
                    ins = nc.tensor.transpose(bank[5 + k // 4][0:27, 128 * (k % 4):128 * (k % 4) + 128],
                                              tail_cols[:, k, :], ident)
                    if k % 4 == 3:
                        ins.then_inc(tail_psum, 1)
                    else:
                        pay(ins)

                pe.wait_ge(dta_ready, l + 1)
                pe.wait_ge(tail_ready, 2 * (l + 1))
                for i, (t0, n) in enumerate(TILES):
                    mm(bank[6][0:8, UPPER[i][0]:NT], dta[0:n, i, :], upper[0:n, UOFF[i]:UOFF[i] + NT - t0], start=(i == 0), stop=(i == 2), skip_group_check=True)
                for j, (j0, nj) in enumerate(TILES):
                    for i in range(j + 1):
                        n = TILES[i][1]
                        c0 = UOFF[i] + j0 - UPPER[i][0]
                        mm(bank[5][0:nj, 8 * j:8 * j + 8], upper[0:n, c0:c0 + nj], dta[0:n, i, :], start=(i == 0), stop=(i == j))
                for j, (j0, nj) in enumerate(TILES):
                    for i in range(j, 3):
                        n = TILES[i][1]
                        c0 = LOFF[i] + j0
                        ins = mm(bank[5][0:nj, 24 + 8 * j:32 + 8 * j], lower[0:n, c0:c0 + nj], dta[0:n, i, :], start=(i == j), stop=(i == 2))
                ins.then_inc(cs_psum, 1)

                pe.wait_ge(xbc_ready, 8 * (l + 1))
                pe.wait_ge(proj_z, 4 * (l + 1))
                pe.wait_ge(qk_ready, 5 * (l + 1))
                for i, (t0, n) in enumerate(TILES):
                    for k in range(4):
                        ins = nc.tensor.transpose(bank[1 + i][0:n, 128 * k:128 * k + 128], xbc[:, k, t0:t0 + n], ident)
                    ins.then_inc(tok_psum, 1)
                for where, w0, k, i in ((4, 0, 4, 0), (4, 128, 5, 0), (4, 256, 4, 1), (4, 384, 5, 1), (7, 0, 4, 2), (7, 128, 5, 2)):
                    t0, n = TILES[i]
                    ins = nc.tensor.transpose(bank[where][0:n, w0:w0 + 128], xbc[:, k, t0:t0 + n], ident)
                    if w0 == 384 or (where == 7 and w0 == 128):
                        ins.then_inc(tok_psum, 1)
                for where, w0, i in ((7, 256, 0), (7, 384, 1), (0, 0, 2)):
                    t0, n = TILES[i]
                    nc.tensor.transpose(bank[where][0:n, w0:w0 + 128], qk[:, 0, t0:t0 + n], ident).then_inc(tok_psum, 1)

                def scores(hd):
                    c, g = hd // 2, hd % 2
                    h = slice(64 * g, 64 * g + 64)
                    A, B = (bank[1], bank[2]) if hd % 2 == 0 else (bank[3], bank[4])
                    if hd >= 2:
                        pe.wait_ge(negmax_ready, 8 * l + hd - 1)
                    q, k = qk[h, 1 + c, :], qk[h, 0, :]
                    mm(A[:, 0:128], q[:, 0:128], k[:, 0:128], start=True, stop=True)
                    mm(A[:, 128:384], q[:, 128:256], k[:, 0:256], start=True, stop=True)
                    mm(B[0:NP - 256, 0:NP], q[:, 256:NP], k[:, 0:NP], start=True, stop=True).then_inc(score_psum, 1)

                def turn_probs(hd):
                    P, T = probs_of[hd % 3], bank[5 + hd % 2]
                    pe.wait_ge(prob_ready, 8 * l + hd + 1)
                    if hd >= 2:
                        pe.wait_ge(probT_ready, 8 * l + hd - 1)
                    tr = nc.tensor.transpose
                    tr(T[:, 0:128], P[:, 0:128], ident)
                    tr(T[:, 128:256], P[:, 128:256], ident)
                    tr(T[:, 256:272], P[0:16, 384:512], ident[0:16, 0:16])
                    tr(T[:, 272:400], P[:, 256:384], ident)
                    tr(T[:, 400:416], P[0:16, 512:640], ident[0:16, 0:16])
                    tr(T[0:16, 416:432], P[0:16, 640:656], ident[0:16, 0:16]).then_inc(probT_psum, 1)

                def attend(hd):
                    c, g = hd // 2, hd % 2
                    h = slice(64 * g, 64 * g + 64)
                    PT = probsT_of[hd % 2]
                    pe.wait_ge(probT_ready, 8 * l + hd + 1)
                    if g == 0 and c >= 2:
                        pe.wait_ge(att_ready, 4 * l + c - 1)
                    out = bank[(7, 0)[c % 2]]
                    mm(out[h, 0:NP], vtok[:, 0, h], PT[:, 0:272], start=True, stop=False)
                    mm(out[h, 128:NP], vtok[:, 1, h], PT[:, 272:416], start=False, stop=False)
                    ins = mm(out[h, 256:NP], vtok[0:16, 2, h], PT[0:16, 416:432], start=False, stop=True)
                    if g == 1:
                        ins.then_inc(att_psum, 1)

                def sample_attention(half):
                    n = 2 * l + half
                    pe.wait_ge(caches_here, 64 * (n + 1))
                    if half:
                        pe.wait_ge(negmax_ready, 8 * (l + 1))
                        pe.wait_ge(probT_ready, 8 * (l + 1))
                    for b in range(4):
                        nc.tensor.transpose(bank[1][:, 128 * b:128 * b + 128], winK[:, b, :], ident)
                    nc.tensor.transpose(bank[2][:, 0:64], metK[0:64, :], ident[0:64, 0:64]).then_inc(s_KT_psum, 1)
                    pe.wait_ge(s_KT_ready, n + 1)
                    pe.wait_ge(qs_ready, l + 1)
                    for g in range(2):
                        h = slice(64 * g, 64 * g + 64)
                        for b in range(4):
                            t0 = NP + 8 * (4 * half + b)
                            q, r = qs[h, 4 * half + b, :, :].rearrange("p c t -> p (c t)"), slice(32 * b, 32 * b + 32)
                            out = bank[(3, 2)[g]][r, 0:152]
                            mm(out[:, 0:128], q, winKT[h, 128 * b:128 * b + 128], start=True, stop=True)
                            mm(out[:, 128:144], q, metKT[h, 16 * b:16 * b + 16], start=True, stop=True)
                            ins = mm(out[:, 144:152], q, qk[h, 0, t0:t0 + ST], start=True, stop=True)
                    ins.then_inc(s_score_psum, 1)
                    pe.wait_ge(s_prob_ready, n + 1)
                    for g in range(2):
                        nc.tensor.transpose(bank[4][:, 128 * g:128 * g + 128], sprob[:, g, 0:128], ident)
                        ins = nc.tensor.transpose(bank[4][0:24, 256 + 128 * g:384 + 128 * g], sprob[:, g, 128:152], ident)
                    ins.then_inc(s_probT_psum, 1)
                    pe.wait_ge(s_probT_ready, n + 1)
                    pe.wait_ge(mnv_new_here, 64 * (n + 1))
                    for b in range(4):
                        for g in range(2):
                            h = slice(64 * g, 64 * g + 64)
                            cols = slice(32 * b, 32 * b + 32)
                            mm(bank[5][h, cols], winV[:, b, h], sprobT[:, 128 * g + 32 * b:128 * g + 32 * b + 32], start=True, stop=False)
                            ins = mm(bank[5][h, cols], mnV[0:24, b, h], sprobT[0:24, 256 + 128 * g + 32 * b:256 + 128 * g + 32 * b + 32], start=False, stop=True)
                    ins.then_inc(s_att_psum, 1)

                pe.wait_ge(tok_ready, 8 * (l + 1))
                pe.wait_ge(cs_ready, l + 1)
                pe.wait_ge(wdec_ready, l + 1)
                sample_attention(0)
                scores(0)
                scores(1)
                pe.wait_ge(s_att_ready, 2 * l + 1)
                turn_probs(0)
                for hd in range(HEADS):
                    if hd + 2 < HEADS:
                        scores(hd + 2)
                    if hd + 1 < HEADS:
                        turn_probs(hd + 1)
                    attend(hd)
                sample_attention(1)
                pe.wait_ge(mixsq_ready, 3 * l + 1)
                for c in range(4):
                    ins = mm(bank[6][:, 0:NT], ones[:, :], conv[:, c, 0:NT], start=(c == 0), stop=(c == 3))
                ins.then_inc(mixsum_psum, 1)

                def pairs_of_tokens(g):
                    for j, (j0, nj) in enumerate(TILES):
                        out = bank[1][0:nj, 0:NT] if j == 0 else bank[2][0:nj, UOFF[j] - NT:UOFF[j] - NT + NT - j0]
                        ins = mm(out, xbc[:, 4 + g, j0:j0 + nj], xbc[:, 6 + g, j0:NT], start=True, stop=True)
                    ins.then_inc(cb_psum, 1)

                def row_decays(pr):
                    for h in (2 * pr, 2 * pr + 1):
                        if h >= 2:
                            pe.wait_ge(seg_ready, 8 * l + h - 1)
                        mm(bank[3 + h % 2][:, 0:NT], ident[0:8, h:h + 1].to_broadcast([8, 128]), csrow, start=True, stop=True).then_inc(seg_psum, 1)

                pe.wait_ge(s_probT_ready, 2 * (l + 1))
                pairs_of_tokens(0)
                row_decays(0)
                for pr in range(4):
                    n, g = 4 * l + pr, pr // 2
                    if pr < 3:
                        row_decays(pr + 1)
                    pe.wait_ge(cb_ready, 2 * l + g + 1)
                    if pr:
                        pe.wait_ge(h0T_ready, 2 * n)
                    pe.wait_ge(h0_here[n % 2], 16 * (n // 2 + 1))
                    for b in range(SB):
                        ins = nc.tensor.transpose(bank[1 + b // 4][:, 128 * (b % 4):128 * (b % 4) + 128], h0[n % 2][:, b, :], ident)
                        if b % 4 == 3:
                            ins.then_inc(h0T_psum, 1)
                    if pr:
                        pe.wait_ge(y_ready, 3 * n)
                        pe.wait_ge(pstate_ready, n)
                    else:
                        pe.wait_ge(att_ready, 4 * (l + 1))
                    for hh in range(2):
                        h = 2 * pr + hh
                        mm(bank[7][64 * hh:64 * hh + 64, 0:64], ident[0:8, h:h + 1].to_broadcast([8, 64]), csrow[:, NP:NT], start=True, stop=True)
                    pe.wait_ge(h0T_ready, 2 * (n + 1))
                    for b in range(SB):
                        ins = mm(bank[7][:, 64 + 8 * b:72 + 8 * b], h0T[:, b, :], xbc[:, 6 + g, NP + 8 * b:NP + 8 * b + 8], start=True, stop=True)
                    ins.then_inc(yoff_psum, 1)
                    if pr >= 2:
                        pe.wait_ge(y_ready, 3 * (4 * l + pr - 1))
                    elif pr == 0:
                        pe.wait_ge(s_att_ready, 2 * (l + 1))
                    else:
                        pe.wait_ge(mixrstd_ready, 3 * l + 1)
                    for hh in range(2):
                        h = 2 * pr + hh
                        pe.wait_ge(M_ready, 8 * l + h + 1)
                        for j, (j0, nj) in enumerate(TILES):
                            ins = mm(bank[5 + pr % 2][64 * hh:64 * hh + 64, j0:NT], xdt[0:nj, j, 64 * h:64 * h + 64],
                                     decay[h % 4][0:nj, UOFF[j]:UOFF[j] + NT - j0], start=(j == 0), stop=(j == 2))
                    ins.then_inc(ydiag_psum, 1)
                    if pr == 1:
                        pairs_of_tokens(1)
                    pe.wait_ge(xw_ready, n + 1)
                    pe.wait_ge(y_ready, 3 * n + 1)
                    for j, nj in ((0, 128), (1, 128), (2, NP - 256)):
                        ins = mm(bank[7][:, 128:256], xw[0:nj, j, :], Btok[0:nj, j, 128 * g:128 * g + 128], start=(j == 0), stop=(j == 2))
                    ins.then_inc(pstate_psum, 1)
                    pe.wait_ge(Bexp_ready, 2 * l + g + 1)
                    for q in range(2):
                        if n or q:
                            pe.wait_ge(sstate_ready, 2 * n + q)
                        mm(bank[0][:, :], xw[0:80, 2, :], Bexp[0:80, 4 * q:4 * q + 4, :], start=True, stop=True).then_inc(sstate_psum, 1)
                for g in range(2):
                    pe.wait_ge(mixsq_ready, 3 * l + 2 + g)
                    for c in (2 * g, 2 * g + 1):
                        ins = mm(bank[1 + g][:, 0:NT], ones[:, :], conv[:, c, 0:NT], start=(c % 2 == 0), stop=(c % 2 == 1))
                    ins.then_inc(mixsum_psum, 1)
                pe.wait_ge(mix_ready, 8 * (l + 1))
                for i in range(DK):
                    wait_slab(pe, s0 + IN_SLABS + i // 2)
                    w = sl(IN_SLABS + i // 2)
                    if i >= 4:
                        pe.wait_ge(xT_ready, 8 + 16 * l + i - 3)
                    for k in range(DK):
                        ins = mm(bank[3 + i % 4][:, 0:NT], w[:, k, 128 * (i % 2):128 * (i % 2) + 128], mixT[:, k, :], start=(k == 0), stop=(k == DK - 1))
                        if k < DK - 1:
                            pay(ins)
                    ins.then_inc(out_psum, 1)
                    owed[0] += i % 2

                norm_sums(2 * l + 1)
                if l == 0:
                    f0 = IN_SLABS + OUT_SLABS
                    for f in range(FC):
                        for w in range(2):
                            n = f0 + 2 * (f // 2) + w
                            wait_slab(pe, n)
                            s = slab(n).rearrange("p (k n) -> p k n", k=DK)
                            if f >= 2:
                                pe.wait_ge(hid_ready, f - 1)
                            else:
                                pe.wait_ge(xT_ready, 16)
                            for k in range(DK):
                                if f == 0 and w == 0:
                                    pe.wait_ge(hn_ready, 8 + k + 1)
                                ins = mm(bank[1 + 2 * w + f % 2][:, 0:NT], s[:, k, 128 * (f % 2):128 * (f % 2) + 128], hnT[:, k, :], start=(k == 0), stop=(k == DK - 1))
                                if k < DK - 1:
                                    pay(ins)
                            ins.then_inc(gu_psum, 1)
                            owed[0] += f % 2
                    for half in range(2):
                        for f in range(FC):
                            blk = half * FC + f
                            n = f0 + GU_SLABS + blk // 4
                            wait_slab(pe, n)
                            s = slab(n).rearrange("p (j n) -> p j n", j=4)[:, blk % 4, :]
                            pe.wait_ge(hid_ready, f + 1)
                            for i in range(4):
                                if half and f == 0:
                                    pe.wait_ge(xT_ready, 16 + i + 1)
                                if blk == 0 and i == 3:
                                    pe.wait_ge(hid_ready, FC - 1)
                                ins = mm(bank[(5, 6, 7, 1)[i]][:, 0:NT], s[:, 128 * i:128 * i + 128], hidT[:, f, :], start=(f == 0), stop=(f == FC - 1))
                                if f == FC - 1:
                                    ins.then_inc(down_psum, 1)
                                else:
                                    pay(ins)
                            owed[0] += blk % 4 == 3

            pe.wait_ge(router_here, 16)
            pe.wait_ge(hn_ready, 32)
            for i, (t0, n) in enumerate(TILES):
                for k in range(DK):
                    ins = mm(bank[1][0:n, 8 * i:8 * i + 8], hnT[:, k, t0:t0 + n], wr[:, k, :], start=(k == 0), stop=(k == DK - 1))
            ins.then_inc(logit_psum, 1)
            pe.wait_ge(xT_ready, 32)
            for src, done, signal in ((hnT, None, turn_psum), (xT, turn_act, comb_psum)):
                for u in range(6):
                    i, half = u // 2, u % 2
                    t0, n = TILES[i]
                    if done is not None:
                        pe.wait_ge(done, u + 1)
                    for q in range(4):
                        ins = nc.tensor.transpose(bank[2 + u][0:n, 128 * q:128 * q + 128], src[:, 4 * half + q, t0:t0 + n], ident)
                    ins.then_inc(signal, 1)
            pe.wait_ge(picks_counted, 1)
            m = R(0)
            for j in range(3):
                nj = TILES[j][1]
                for i in range(j + 1):
                    n = TILES[i][1]
                    tri = upper[0:n, UOFF[1]:UOFF[1] + nj] if i == j else ones[0:n, 0:nj]
                    mm(bank[1][0:nj, 32 + 8 * j:40 + 8 * j], tri, m[0:n, i, :], start=(i == 0), stop=(i == j))
            for i in range(3):
                n = TILES[i][1]
                ins = mm(bank[1][:, 64:72], ones[0:n, :], m[0:n, i, :], start=(i == 0), stop=(i == 2))
            ins.then_inc(count_psum, 1)
            pe.wait_ge(comb_added, 6)
            pe.wait_ge(route_ready, 1)

            def gather(k):
                pe.wait_ge(pick_ready, k + 1)
                for c in range(DK):
                    for i, (t0, n) in enumerate(TILES):
                        ins = mm(bank[c // 4][:, SLOTS * (c % 4):SLOTS * (c % 4) + SLOTS], hn_tok[0:n, i, 128 * c:128 * c + 128], pick[0:n, i, :], start=(i == 0), stop=(i == 2))
                        if i < 2:
                            pay(ins)
                    if c % 4 == 3:
                        ins.then_inc(xg_psum, 1)
                if k is not first_pass:
                    pe.wait_ge(pickT_ready, k)
                for i, (t0, n) in enumerate(TILES):
                    ins = nc.tensor.transpose(bank[2][0:SLOTS, t0:t0 + n], gpick[0:n, i, :], ident[0:n, 0:n])
                ins.then_inc(pickT_psum, 1)

            def expert_pass(k):
                pe.wait_ge(xg_ready, 2 * k + 2)
                for f in range(FC):
                    for w in range(2):
                        j = 2 * (f // 2) + w
                        s = (MOE0 + j) % RING
                        if f % 2 == 0:
                            pe.wait_ge(slab_here[s], k * (16 * FFN_SLABS // RING) + (fixed_seen[s] + 16 * (j // RING + 1)))
                        if w == 0:
                            pe.wait_ge(hid_ready, k * FC + (FC + f - 1))
                        for c in range(DK):
                            ins = mm(bank[3 + f % 2][:, SLOTS * w:SLOTS * w + SLOTS], slots[s].rearrange("p (k n) -> p k n", k=DK)[:, c, 128 * (f % 2):128 * (f % 2) + 128],
                                     xg[:, c, :], start=(c == 0), stop=(c == DK - 1))
                            if c < DK - 1:
                                pay(ins)
                        owed[0] += f % 2
                        if w == 1:
                            ins.then_inc(gu_psum, 1)
                for f in range(FC):
                    j = GU_SLABS + f // 2
                    s = (MOE0 + j) % RING
                    if f % 2 == 0:
                        pe.wait_ge(slab_here[s], k * (16 * FFN_SLABS // RING) + (fixed_seen[s] + 16 * (j // RING + 1)))
                    pe.wait_ge(hid_ready, k * FC + (FC + f + 1))
                    if f == 0:
                        pe.wait_ge(comb_added, 6 * k + 6)
                    for half in range(2):
                        ins = mm(bank[5 + half][0:SLOTS, :], hid[:, f, :], slots[s].rearrange("p (r n) -> p r n", r=2)[:, f % 2, 512 * half:512 * half + 512],
                                 start=(f == 0), stop=(f == FC - 1))
                        if f == FC - 1:
                            ins.then_inc(y_psum, 1)
                        else:
                            pay(ins)
                    owed[0] += f % 2
                pe.wait_ge(pickT_ready, k + 1)
                gather(k + 1)
                pe.wait_ge(ytok_ready, 2 * k + 2)
                for u in range(6):
                    i, half = u // 2, u % 2
                    t0, n = TILES[i]
                    if u >= 3:
                        pe.wait_ge(comb_added, 6 * k + (u + 4))
                    mm(bank[5 + u % 3][0:n, :], gpickT[:, t0:t0 + n], ytok[:, 512 * half:512 * half + 512], start=True, stop=True).then_inc(comb_psum, 1)
                assert owed[0] == 0

            gather(first_pass)
            with pe.Fori(0, EXPERTS) as e:
                expert_pass(e)
            fullest = pe.value_load(crowded[0:1, 0:1], min_val=0, max_val=NT)
            with pe.If(fullest > SLOTS):
                with pe.Fori(1, PASSES) as b:
                    with pe.Fori(0, EXPERTS) as e:
                        expert_pass(b * EXPERTS + e)

        @block.scalar
        def _(act):
            step = [0]

            def link(ins):
                step[0] += 1
                ins.then_inc(act_step, 1)
                act.wait_ge(act_step, step[0])

            f = nc.scalar.activation
            with nc.allow_non_contiguous_dma(reason="small tables"):
                prow = conv_[:, 128:256]
                for l in range(LAYERS):
                    r = PARAM_ROWS * l

                    def row(r0, n, src):
                        act.dma_start(prow[r + r0:r + r0 + n, :], src).then_inc(params_here, 16)

                    row(R_MIX, 8, a["norm_mix_w"][l].rearrange("(k p) -> k p", p=128))
                    row(R_FFN, 8, a["norm_ffn_w"][l].rearrange("(k p) -> k p", p=128))
                    row(R_CW, 32, a["conv_w"][l].rearrange("w (k p) -> (w k) p", p=128))
                    row(R_CB, 8, a["conv_b"][l].rearrange("(k p) -> k p", p=128))
                    row(R_SSD, 4, a["ssd_norm_w"][l].rearrange("(k p) -> k p", p=128))
                    for g in range(2):
                        act.dma_start(prow[r + R_ATT:r + R_ATT + 4, 64 * g:64 * g + 64],
                                       a["attn_norm_w"][l][256 * g:256 * g + 256].rearrange("(c d) -> c d", d=64)).then_inc(params_here, 16)


            def norm(n, out):
                for k in range(DK):
                    act.wait_ge(xT_ready, 8 * n + k + 1)
                    f(squares[n % 2][:, k, :], xT[:, k, :], ACT.Square).then_inc(squares_ready, 1)
                act.wait_ge(sum_psum, n + 1)
                link(f(out, bank[0][:, 0:NT], ACT.Ln, scale=1.0 / D, bias=eps))
                f(out, out, ACT.Exp, scale=-0.5).then_inc(rstd_ready, 1)

            for l in range(LAYERS):
                norm(2 * l, rstd)
                for s in range(8):
                    if s < 5:
                        act.wait_ge(proj_dve, 7 * l + 3 + s)
                        if s >= 2:
                            act.wait_ge(qk_ready, 5 * l + s - 1)
                        t = tmp2[s % 2]
                        f(t[:, 0, :], qk[:, s, :], ACT.Square).then_inc(qksq_ready, 1)
                    act.wait_ge(proj_psum, 18 * l + 7 + s)
                    if s == 0:
                        act.wait_ge(prev_ready, l + 1)
                    src = bank[1 + (6 + s) % 4]
                    f(raw[:, s, 3:NP + 3], src[:, 0:NP], ACT.Copy)
                    f(raw[:, s, S0:NPAD].rearrange("p (b t) -> p b t", t=ST + 3)[:, :, 3:ST + 3],
                      src[:, NP:NT].rearrange("p (b t) -> p b t", t=ST), ACT.Copy).then_inc(proj_raw, 1)
                    if s < 5:
                        act.wait_ge(qksum_psum, 5 * l + s + 1)
                        link(f(t[:, 1, :], bank[5 + s % 2][:, 0:NT], ACT.Ln, scale=1.0 / 64, bias=eps))
                        f(t[:, 1, :], t[:, 1, :], ACT.Exp, scale=-0.5).then_inc(qkrstd_ready, 1)
                act.wait_ge(dt_exp_in, l + 1)
                f(nega, alog[l], ACT.Exp)
                f(dw[1], dw[1], ACT.Exp, scale=-1.0).then_inc(dt_exp, 1)
                act.wait_ge(dt_ln_in, l + 1)
                f(dw[3], dw[2], ACT.Ln).then_inc(dt_ln, 1)
                for c in range(4):
                    act.wait_ge(proj_psum, 18 * l + 15 + c)
                    f(zs[:, c, :], bank[1 + (14 + c) % 4][:, 0:NT], ACT.Silu).then_inc(proj_z, 1)
                act.wait_ge(conv_ready, 8 * (l + 1))
                act.wait_ge(tail_psum, 2 * (l + 1))
                for k in range(DK):
                    f(xbc[:, k, 0:NP], conv[:, k, 0:NP], ACT.Silu)
                    f(xbc[:, k, NP:NT].rearrange("p (b t) -> p b t", t=ST),
                      samples_of_conv(conv, k), ACT.Silu).then_inc(xbc_ready, 1)
                act.wait_ge(cs_psum, l + 1)
                act.wait_ge(cs_ready, l + 1)
                f(wdec[:, 0:2, :], bank[5][:, 24:40].rearrange("p (i h) -> p i h", i=2), ACT.Exp)
                f(wdec[0:80, 2, :], bank[5][0:80, 40:48], ACT.Exp).then_inc(wdec_ready, 1)
                def sample_exps(half):
                    act.wait_ge(s_negmax_ready, 2 * l + half + 1)
                    for g in range(2):
                        f(es[0][:, g:g + 1], nm[0][:, g:g + 1], ACT.Exp, bias=sink_s[l][:, g:g + 1])
                        ins = f(sprob[:, g, :], sprob[:, g, :], ACT.Exp, bias=nm[0][:, g:g + 1], accum_out=sums[0][:, g:g + 1])
                    ins.then_inc(s_exp_ready, 1)

                sample_exps(0)
                for hd in range(HEADS):
                    c, g, n = hd // 2, hd % 2, 8 * l + hd
                    P, i = probs_of[hd % 3], hd % 3
                    act.wait_ge(negmax_ready, n + 1)
                    sink = sinks[l][:, c + 4 * g:c + 4 * g + 1]
                    f(es[i], nm[i], ACT.Exp, bias=sink)
                    f(P[:, 0:128], P[:, 0:128], ACT.Exp, bias=nm[i][:, 0:1], accum_out=sums[i][:, 0:1])
                    f(P[:, 128:384], P[:, 128:384], ACT.Exp, bias=nm[i][:, 1:2], accum_out=sums[i][:, 1:2])
                    f(P[0:16, 384:656], P[0:16, 384:656], ACT.Exp, bias=nm[i][0:16, 2:3], accum_out=sums[i][0:16, 2:3]).then_inc(exp_ready, 1)
                sample_exps(1)
                act.wait_ge(att_ready, 4 * (l + 1))
                act.wait_ge(s_att_ready, 2 * (l + 1))
                act.wait_ge(att_psum, 4 * (l + 1))
                f(conv[:, 0:4, 0:NT], mixT[:, 4:8, :], ACT.Square).then_inc(mixsq_ready, 1)
                act.wait_ge(mixsum_psum, 3 * l + 1)
                link(f(rstd_m, bank[6][:, 0:NT], ACT.Ln, scale=1.0 / 512, bias=eps))
                f(rstd_m, rstd_m, ACT.Exp, scale=-0.5).then_inc(mixrstd_ready, 1)
                def decays(pr):
                    for h in (2 * pr, 2 * pr + 1):
                        act.wait_ge(seg_ready, 8 * l + h + 1)
                        f(decay[h % 4][:, 0:UOFF[2]], decay[h % 4][:, 0:UOFF[2]], ACT.Exp)
                        f(decay[h % 4][0:80, UOFF[2]:UCOLS], decay[h % 4][0:80, UOFF[2]:UCOLS], ACT.Exp).then_inc(decay_exp, 1)

                decays(0)
                for pr in range(4):
                    n = 4 * l + pr
                    if pr < 3:
                        decays(pr + 1)
                    act.wait_ge(yoff_psum, n + 1)
                    if n:
                        act.wait_ge(sstate_ready, 2 * n)
                        act.wait_ge(y_ready, 3 * n)
                    f(eoff, bank[7][:, 0:64], ACT.Exp).then_inc(eoff_ready, 1)
                for g in range(2):
                    act.wait_ge(y_ready, 12 * (l + 1))
                    act.wait_ge(mixsum_psum, 3 * l + 1 + g)
                    f(conv[:, 2 * g:2 * g + 2, 0:NT], mixT[:, 2 * g:2 * g + 2, :], ACT.Square).then_inc(mixsq_ready, 1)
                    act.wait_ge(mixsum_psum, 3 * l + 2 + g)
                    act.wait_ge(mix_ready, 8 * l + 4 + 2 * g)
                    link(f(rstd_m, bank[1 + g][:, 0:NT], ACT.Ln, scale=1.0 / 256, bias=eps))
                    f(rstd_m, rstd_m, ACT.Exp, scale=-0.5).then_inc(mixrstd_ready, 1)
                for i in range(2):
                    act.wait_ge(states_stored[i], 64 * (l + 1))
                norm(2 * l + 1, rstd_f)
                if l == 0:
                    for c in range(FC):
                        act.wait_ge(gu_psum, 2 * c + 1)
                        if c >= 2:
                            act.wait_ge(hid_ready, c - 1)
                        f(gate_s[c % 2], bank[1 + c % 2][:, 0:NT], ACT.Silu).then_inc(silu_ready, 1)
            act.wait_ge(gates_in, 1)
            f(R(96, 3, 1)[:, :, 0], R(96, 3, 1)[:, :, 0], ACT.Exp).then_inc(gates_exp, 1)
            for u in range(6):
                i, half = u // 2, u % 2
                n = TILES[i][1]
                act.wait_ge(turn_psum, u + 1)
                f(hn_tok[0:n, i, 512 * half:512 * half + 512], bank[2 + u][0:n, :], ACT.Copy).then_inc(turn_act, 1)

            def gathered(k):
                for half in range(2):
                    act.wait_ge(xg_psum, 2 * k + (half + 1))
                    f(xg_[:, 4 * SLOTS * half:4 * SLOTS * (half + 1)], bank[half][:, 0:4 * SLOTS], ACT.Copy).then_inc(xg_ready, 1)

            def expert_pass(k):
                for c in range(FC):
                    act.wait_ge(gu_psum, k * FC + (2 * FC + c + 1))
                    act.wait_ge(hid_ready, k * FC + (FC + c - 1))
                    f(gsil[c % 2], bank[3 + c % 2][:, 0:SLOTS], ACT.Silu).then_inc(silu_ready, 1)
                act.wait_ge(comb_psum, 6 * k + 6)
                for half in range(2):
                    act.wait_ge(y_psum, 2 * k + (half + 1))
                    f(ytok[:, 512 * half:512 * half + 512], bank[5 + half][0:SLOTS, :], ACT.Copy).then_inc(ytok_ready, 1)
                gathered(k + 1)

            act.wait_ge(route_ready, 1)
            gathered(0)
            with act.Fori(0, EXPERTS) as e:
                expert_pass(e)
            fullest = act.value_load(crowded[0:1, 0:1], min_val=0, max_val=NT)
            with act.If(fullest > SLOTS):
                with act.Fori(1, PASSES) as b:
                    with act.Fori(0, EXPERTS) as e:
                        expert_pass(b * EXPERTS + e)

        @block.vector
        def _(dve):
            v = nc.vector
            step = [0]

            def link(ins):
                step[0] += 1
                ins.then_inc(dve_step, 1)
                dve.wait_ge(dve_step, step[0])

            dve.wait_ge(set_up, 3)
            dve.wait_ge(const_here, 16)
            for k in range(DK):
                dve.wait_ge(xin_psum, k + 1)
                v.tensor_copy(xT[:, k, :], bank[1 + k % 4][:, 0:NT]).then_inc(xT_ready, 1)
            dve.wait_ge(params_psum, 1)
            link(v.tensor_copy(params[:, :], bank[7][:, 0:128]))

            def normed(n, l, r0, scale):
                dve.wait_ge(rstd_ready, n + 1)
                for k in range(DK):
                    c = PARAM_ROWS * l + r0 + k
                    v.scalar_tensor_tensor(out=hnT[:, k, :], in0=xT[:, k, :], scalar=params[:, c:c + 1], in1=scale,
                                           op0=ALU.mult, op1=ALU.mult).then_inc(hn_ready, 1)

            for l in range(LAYERS):
                P0 = PARAM_ROWS * l
                if l:
                    dve.wait_ge(down_psum, 8)
                dve.wait_ge(xT_ready, 8 if l == 0 else 24)
                link(v.memset(raw[:, :, 0:3], 0.0))
                dve.wait_ge(prev_psum, l + 1)
                for r in range(3):
                    ins = v.tensor_copy(raw[:, :, S0 + r:S0 + r + 78:11], bank[1][:, 0:192].rearrange("p (k b r) -> p k b r", k=DK, r=3)[:, :, :, r])
                    (ins.then_inc(prev_ready, 1) if r == 2 else None)
                normed(2 * l, l, R_MIX, rstd)
                if l == 0:
                    dve.wait_ge(small_here, 16 * 9 * LAYERS)
                    for n in range(LAYERS):
                        link(v.tensor_scalar(qkw[2 * n + 1], qkw[2 * n + 1], 0.125, None, ALU.mult))
                dve.wait_ge(proj_psum, 18 * l + 1)
                v.tensor_copy(vtok[:, 0:2, :], bank[1][:, 0:256].rearrange("p (i n) -> p i n", i=2))
                v.tensor_copy(vtok[0:80, 2, :], bank[1][0:80, 256:384]).then_inc(proj_dve, 1)
                raw_dt = dw[0]
                v3 = [w.rearrange("p (i h) -> p i h", i=3) for w in dw]
                v.tensor_tensor(v3[0][:, 0:2, :], bank[1][:, 384:400].rearrange("p (i h) -> p i h", i=2), bc(dtb[l], 1, 2), ALU.add)
                v.tensor_tensor(v3[0][0:80, 2, :], bank[1][0:80, 400:408], dtb[l][0:80, :], ALU.add).then_inc(proj_dve, 1)
                for n in range(5):
                    dve.wait_ge(proj_psum, 18 * l + 2 + n)
                    v.tensor_copy(qk[:, n, :], bank[1 + (1 + n) % 4][:, 0:NT]).then_inc(proj_dve, 1)
                dve.wait_ge(proj_dve, 7 * l + 7)
                link(v.tensor_scalar(dw[1], raw_dt, -1.0, None, ALU.mult))
                v.tensor_tensor(dw[1], dw[1], raw_dt, ALU.max).then_inc(dt_exp_in, 1)

                def conv_chunk(k):
                    dve.wait_ge(proj_raw, 8 * l + k + 1)
                    for w in range(CONV_W):
                        s = params[:, P0 + R_CW + 8 * w + k:P0 + R_CW + 8 * w + k + 1]
                        if w == 0:
                            link(v.tensor_scalar(conv[:, k, 0:NCONV], raw[:, k, 0:NCONV], s, params[:, P0 + R_CB + k:P0 + R_CB + k + 1], ALU.mult, ALU.add))
                        else:
                            ins = v.scalar_tensor_tensor(out=conv[:, k, 0:NCONV], in0=raw[:, k, w:w + NCONV], scalar=s, in1=conv[:, k, 0:NCONV], op0=ALU.mult, op1=ALU.add)
                            if w < CONV_W - 1:
                                link(ins)
                            else:
                                ins.then_inc(conv_ready, 1)

                def turned(n):
                    t = tmp2[n % 2]
                    dve.wait_ge(rot_psum, 5 * l + n + 1)
                    link(v.tensor_tensor(t[:, 2, :], bank[(7, 0)[n % 2]][:, 0:NT], sinT, ALU.mult))
                    link(v.tensor_tensor(qk[:, n, :], qk[:, n, :], cosT, ALU.mult))
                    v.tensor_tensor(qk[:, n, :], qk[:, n, :], t[:, 2, :], ALU.add).then_inc(qk_ready, 1)

                for s in range(8):
                    if s < 5:
                        dve.wait_ge(qkrstd_ready, 5 * l + s + 1)
                        w = qkw[2 * l + (1 if s else 0)]
                        v.scalar_tensor_tensor(out=qk[:, s, :], in0=qk[:, s, :], scalar=w, in1=tmp2[s % 2][:, 1, :], op0=ALU.mult, op1=ALU.mult).then_inc(qkn_ready, 1)
                    conv_chunk(s)
                    if 1 <= s <= 5:
                        turned(s - 1)
                for k in range(DK):
                    ins = v.tensor_copy(tail_cols[:, k, :].rearrange("p (j r) -> p j r", r=3), tail_view(raw, k))
                ins.then_inc(tail_cols_ready, 1)
                dve.wait_ge(qk_ready, 5 * (l + 1))
                for c in range(4):
                    ins = v.tensor_copy(qs[:, :, c, :], qk[:, 1 + c, NP:NT].rearrange("p (b t) -> p b t", t=ST))
                ins.then_inc(qs_ready, 1)
                dve.wait_ge(dt_exp, l + 1)
                v.tensor_scalar(dw[2], dw[1], 1.0, None, ALU.add).then_inc(dt_ln_in, 1)
                dve.wait_ge(dt_ln_in, l + 1)
                link(v.tensor_scalar(dw[4], dw[2], -1.0, 1e-30, ALU.add, ALU.max))
                link(v.reciprocal(dw[4], dw[4]))
                link(v.tensor_tensor(dw[4], dw[4], dw[1], ALU.mult))
                dve.wait_ge(dt_ln, l + 1)
                link(v.tensor_tensor(dw[4], dw[4], dw[3], ALU.mult))
                link(v.tensor_scalar(dw[3], dw[2], 1.0, None, ALU.is_equal))
                link(v.tensor_tensor(dw[3], dw[3], dw[1], ALU.mult))
                link(v.tensor_tensor(dw[4], dw[4], dw[3], ALU.add))
                link(v.scalar_tensor_tensor(out=dt.rearrange("p i h -> p (i h)"), in0=raw_dt, scalar=0.0, in1=dw[4], op0=ALU.max, op1=ALU.add))
                link(v.tensor_tensor(dta, dt, bc(nega, 1, 3), ALU.mult))
                v.tensor_scalar(dta, dta, -1.0, None, ALU.mult).then_inc(dta_ready, 1)
                for h in range(2):
                    dve.wait_ge(tail_psum, 2 * l + h + 1)
                    v.tensor_copy(tails[0:27, 512 * h:512 * h + 512], bank[5 + h][0:27, :]).then_inc(tail_ready, 1)
                dve.wait_ge(cs_psum, l + 1)
                v.tensor_copy(csrow, bank[6][0:8, 0:NT])
                v.tensor_scalar(negcs[:, 0:2, :], bank[5][:, 0:16].rearrange("p (i h) -> p i h", i=2), -1.0, None, ALU.mult)
                v.tensor_scalar(negcs[0:80, 2, :], bank[5][0:80, 16:24], -1.0, None, ALU.mult).then_inc(cs_ready, 1)
                for i, (t0, n) in enumerate(TILES):
                    dve.wait_ge(tok_psum, 8 * l + i + 1)
                    v.tensor_tensor(xdt[0:n, i, :].rearrange("p (h d) -> p h d", h=HEADS), bank[1 + i][0:n, :].rearrange("p (h d) -> p h d", h=HEADS),
                                    bc(dt[0:n, i, :], 2, 64), ALU.mult).then_inc(tok_ready, 1)
                dve.wait_ge(tok_psum, 8 * l + 4)
                v.tensor_copy(Btok[:, 0:2, :], bank[4][:, :].rearrange("p (i n) -> p i n", i=2)).then_inc(tok_ready, 1)
                dve.wait_ge(tok_psum, 8 * l + 7)
                v.tensor_copy(Btok[0:80, 2, :], bank[7][0:80, 0:256]).then_inc(tok_ready, 1)
                for n, (src, i) in enumerate(((bank[7][:, 256:384], 0), (bank[7][:, 384:512], 1), (bank[0][0:80, 0:128], 2))):
                    dve.wait_ge(tok_psum, 8 * l + 6 + n)
                    v.tensor_copy(ktok[0:src.shape[0], i, :], src).then_inc(tok_ready, 1)

                def masked(hd):
                    c, g, i = hd // 2, hd % 2, hd % 3
                    A, B = (bank[1], bank[2]) if hd % 2 == 0 else (bank[3], bank[4])
                    P = probs_of[i]
                    dve.wait_ge(score_psum, 8 * l + hd + 1)
                    if hd >= 3:
                        dve.wait_ge(probT_psum, 8 * l + hd - 2)
                    v.tensor_tensor(P[:, 0:128], A[:, 0:128], C("mask0"), ALU.add)
                    v.tensor_tensor(P[:, 128:384], A[:, 128:384], C("mask1"), ALU.add)
                    link(v.tensor_tensor(P[0:16, 384:656], B[0:16, 0:NP], C("mask2")[0:16, :], ALU.add))
                    v.tensor_reduce(mx[i][:, 0:1], P[:, 0:128], AX.X, ALU.max)
                    v.tensor_reduce(mx[i][:, 1:2], P[:, 128:384], AX.X, ALU.max)
                    link(v.tensor_reduce(mx[i][0:16, 2:3], P[0:16, 384:656], AX.X, ALU.max))
                    v.tensor_scalar(nm[i], mx[i], sinks[l][:, c + 4 * g:c + 4 * g + 1], -1.0, ALU.max, ALU.mult).then_inc(negmax_ready, 1)

                def probs(hd):
                    i = hd % 3
                    P = probs_of[i]
                    dve.wait_ge(exp_ready, 8 * l + hd + 1)
                    link(v.tensor_tensor(sums[i], sums[i], es[i], ALU.add))
                    link(v.reciprocal(sums[i], sums[i]))
                    v.tensor_scalar(P[:, 0:128], P[:, 0:128], sums[i][:, 0:1], None, ALU.mult)
                    v.tensor_scalar(P[:, 128:384], P[:, 128:384], sums[i][:, 1:2], None, ALU.mult)
                    v.tensor_scalar(P[0:16, 384:656], P[0:16, 384:656], sums[i][0:16, 2:3], None, ALU.mult).then_inc(prob_ready, 1)

                def probsT(hd):
                    PT, T = probsT_of[hd % 2], bank[5 + hd % 2]
                    dve.wait_ge(probT_psum, 8 * l + hd + 1)
                    v.tensor_copy(PT[:, 0:416], T[:, 0:416])
                    v.tensor_copy(PT[0:16, 416:432], T[0:16, 416:432]).then_inc(probT_ready, 1)

                def attended(c):
                    dve.wait_ge(att_psum, 4 * l + c + 1)
                    v.tensor_copy(mixT[:, 4 + c, 0:NP], bank[(7, 0)[c % 2]][:, 0:NP]).then_inc(att_ready, 1)

                def sample_attention(half):
                    n = 2 * l + half
                    dve.wait_ge(s_KT_psum, n + 1)
                    v.tensor_copy(winKT, bank[1][:, :])
                    v.tensor_copy(metKT, bank[2][:, 0:64]).then_inc(s_KT_ready, 1)
                    dve.wait_ge(s_score_psum, n + 1)
                    dve.wait_ge(sinks_here, 16 * 16 * (l + 1))
                    v.tensor_tensor(sprob[:, 0, :], bank[3][:, 0:152], C("mask_s"), ALU.add)
                    link(v.tensor_tensor(sprob[:, 1, :], bank[2][:, 0:152], C("mask_s"), ALU.add))
                    link(v.tensor_reduce(mx[0][:, 0:2], sprob, AX.X, ALU.max))
                    link(v.tensor_tensor(mx[0][:, 0:2], mx[0][:, 0:2], sink_s[l], ALU.max))
                    v.tensor_scalar(nm[0][:, 0:2], mx[0][:, 0:2], -1.0, None, ALU.mult).then_inc(s_negmax_ready, 1)
                    dve.wait_ge(s_exp_ready, n + 1)
                    link(v.tensor_tensor(sums[0][:, 0:2], sums[0][:, 0:2], es[0][:, 0:2], ALU.add))
                    link(v.reciprocal(sums[0][:, 0:2], sums[0][:, 0:2]))
                    v.tensor_scalar(sprob[:, 0, :], sprob[:, 0, :], sums[0][:, 0:1], None, ALU.mult)
                    v.tensor_scalar(sprob[:, 1, :], sprob[:, 1, :], sums[0][:, 1:2], None, ALU.mult).then_inc(s_prob_ready, 1)
                    dve.wait_ge(s_probT_psum, n + 1)
                    v.tensor_copy(sprobT[:, 0:256], bank[4][:, 0:256])
                    v.tensor_copy(sprobT[0:24, 256:512], bank[4][0:24, 256:512]).then_inc(s_probT_ready, 1)
                    dve.wait_ge(s_att_psum, n + 1)
                    t0 = NP + 32 * half
                    for c in range(4):
                        ins = v.tensor_copy(mixT[:, 4 + c, t0:t0 + 32].rearrange("p (b t) -> p b t", t=ST),
                                            bank[5][:, 0:128].rearrange("p (b c t) -> p b c t", b=4, c=4)[:, :, c, :])
                    ins.then_inc(s_att_ready, 1)

                dve.wait_ge(proj_psum, 18 * (l + 1))
                dve.wait_ge(xbc_ready, 8 * (l + 1))
                sample_attention(0)
                masked(0)
                masked(1)
                probs(0)
                for hd in range(HEADS):
                    if hd + 2 < HEADS:
                        masked(hd + 2)
                    if hd + 1 < HEADS:
                        probs(hd + 1)
                    probsT(hd)
                    if hd % 2 == 0 and hd:
                        attended(hd // 2 - 1)
                attended(3)
                sample_attention(1)

                def mixed(n, chunks, r0):
                    dve.wait_ge(mixrstd_ready, n)
                    for c in chunks:
                        p = P0 + r0 + c % 4
                        v.scalar_tensor_tensor(out=mixT[:, c, :], in0=mixT[:, c, :], scalar=params[:, p:p + 1], in1=rstd_m,
                                               op0=ALU.mult, op1=ALU.mult).then_inc(mix_ready, 1)

                mixed(3 * l + 1, range(4, 8), R_ATT)
                def token_pairs(g):
                    dve.wait_ge(cb_psum, 2 * l + g + 1)
                    v.tensor_tensor(cbm[:, 0:NT], bank[1][:, 0:NT], upper[:, 0:NT], ALU.mult)
                    v.tensor_tensor(cbm[:, NT:UOFF[2]], bank[2][:, 0:NT - 128], upper[:, NT:UOFF[2]], ALU.mult)
                    v.tensor_tensor(cbm[0:80, UOFF[2]:UCOLS], bank[2][0:80, NT - 128:NT - 128 + 80], upper[0:80, UOFF[2]:UCOLS], ALU.mult).then_inc(cb_ready, 1)

                def batch_blocks(g):
                    v.tensor_tensor(Bexp[0:80, :, :], bc(Btok[0:80, 2, 128 * g:128 * g + 128], 1, SB), bc(C("batch")[0:80, :], 2, 128), ALU.mult).then_inc(Bexp_ready, 1)

                def clamped(pr):
                    if pr >= 2:
                        dve.wait_ge(ydiag_psum, 4 * l + pr - 1)
                    for h in (2 * pr, 2 * pr + 1):
                        dve.wait_ge(seg_psum, 8 * l + h + 1)
                        for j, (j0, nj) in enumerate(TILES):
                            ins = v.tensor_scalar(decay[h % 4][0:nj, UOFF[j]:UOFF[j] + NT - j0], bank[3 + h % 2][0:nj, j0:NT],
                                                  negcs[0:nj, j, h:h + 1], 0.0, ALU.add, ALU.min)
                        ins.then_inc(seg_ready, 1)

                token_pairs(0)
                clamped(0)
                dve.wait_ge(kv_stored, 32 * (l + 1))
                batch_blocks(0)
                dve.wait_ge(wdec_ready, l + 1)
                for pr in range(4):
                    n, g = 4 * l + pr, pr // 2
                    if pr < 3:
                        clamped(pr + 1)
                    for half in range(2):
                        dve.wait_ge(h0T_psum, 2 * n + half + 1)
                        if pr and half == 0:
                            dve.wait_ge(yoff_psum, n)
                        v.tensor_copy(h0T_[:, 512 * half:512 * half + 512], bank[1 + half][:, :]).then_inc(h0T_ready, 1)
                    dve.wait_ge(cb_ready, 2 * l + g + 1)
                    for h in (2 * pr, 2 * pr + 1):
                        dve.wait_ge(decay_exp, 8 * l + h + 1)
                        v.tensor_tensor(decay[h % 4][:, 0:UOFF[2]], decay[h % 4][:, 0:UOFF[2]], cbm[:, 0:UOFF[2]], ALU.mult)
                        v.tensor_tensor(decay[h % 4][0:80, UOFF[2]:UCOLS], decay[h % 4][0:80, UOFF[2]:UCOLS], cbm[0:80, UOFF[2]:UCOLS], ALU.mult).then_inc(M_ready, 1)
                    if pr:
                        dve.wait_ge(sstate_psum, 2 * n)
                    if pr == 2:
                        batch_blocks(1)
                    cols = slice(128 * pr, 128 * pr + 128)
                    for i, (t0, nn) in enumerate(TILES):
                        ins = v.tensor_tensor(xw[0:nn, i, :].rearrange("p (h d) -> p h d", h=2), xdt[0:nn, i, cols].rearrange("p (h d) -> p h d", h=2),
                                              bc(wdec[0:nn, i, 2 * pr:2 * pr + 2], 2, 64), ALU.mult)
                    ins.then_inc(xw_ready, 1)
                    y = mixT[:, pr, :]
                    dve.wait_ge(eoff_ready, n + 1)
                    link(v.tensor_tensor(yoff, bank[7][:, 64:128], eoff, ALU.mult))
                    dve.wait_ge(ydiag_psum, n + 1)
                    v.scalar_tensor_tensor(out=y, in0=xbc[:, pr, :], scalar=dskip[l][:, pr:pr + 1], in1=bank[5 + pr % 2][:, 0:NT], op0=ALU.mult, op1=ALU.add).then_inc(y_ready, 1)
                    dve.wait_ge(y_ready, 3 * n + 1)
                    v.tensor_tensor(y[:, NP:NT], y[:, NP:NT], yoff, ALU.add).then_inc(y_ready, 1)
                    dve.wait_ge(y_ready, 3 * n + 2)
                    v.tensor_tensor(y, y, zs[:, pr, :], ALU.mult).then_inc(y_ready, 1)
                    if pr == 1:
                        token_pairs(1)
                    hp, hp_ = h0[n % 2], h0_[n % 2]
                    link(v.tensor_tensor(hp, hp, bc(eoff[:, 7:64:8], 2, 128), ALU.mult))
                    dve.wait_ge(pstate_psum, n + 1)
                    if n >= 2:
                        dve.wait_ge(states_stored[n % 2], 32 * (n // 2))
                    v.tensor_copy(pst[n % 2], bank[7][:, 128:256]).then_inc(pstate_ready, 1)
                    for q in range(2):
                        dve.wait_ge(sstate_psum, 2 * n + q + 1)
                        v.tensor_tensor(hp_[:, 512 * q:512 * q + 512], hp_[:, 512 * q:512 * q + 512], bank[0][:, :], ALU.add).then_inc(sstate_ready, 1)
                for g in range(2):
                    mixed(3 * l + 2 + g, (2 * g, 2 * g + 1), R_SSD)
                for i in range(DK):
                    dve.wait_ge(out_psum, 8 * l + i + 1)
                    v.tensor_tensor(xT[:, i, :], xT[:, i, :], bank[3 + i % 4][:, 0:NT], ALU.add).then_inc(xT_ready, 1)
                normed(2 * l + 1, l, R_FFN, rstd_f)
                if l == 0:
                    for i in range(2):
                        dve.wait_ge(states_stored[i], 64)
                    dve.wait_ge(outputs_stored, 16 * (2 + 2 * (3 + SB)))
                    for c in range(FC):
                        dve.wait_ge(silu_ready, c + 1)
                        dve.wait_ge(gu_psum, 2 * c + 2)
                        v.tensor_tensor(hidT[:, c, :], gate_s[c % 2], bank[3 + c % 2][:, 0:NT], ALU.mult).then_inc(hid_ready, 1)
                    for i in range(DK):
                        dve.wait_ge(down_psum, i + 1)
                        v.tensor_tensor(xT[:, i, :], xT[:, i, :], bank[(5, 6, 7, 1)[i % 4]][:, 0:NT], ALU.add).then_inc(xT_ready, 1)

            for i in range(2):
                dve.wait_ge(states_stored[i], 64 * LAYERS)
            dve.wait_ge(outputs_stored, 16 * LAYERS * (2 + 2 * (3 + SB)))
            link(v.memset(route[:, 0:400], 0.0))
            dve.wait_ge(logit_psum, 1)
            lg, top, oh1, oh2, gate, mm_ = R(24), R(48), R(104), R(128), R(152), R(0)
            v.tensor_copy(lg[:, 0:2, :], bank[1][:, 0:16].rearrange("p (i e) -> p i e", i=2))
            link(v.tensor_copy(lg[0:80, 2, :], bank[1][0:80, 16:24]))
            for i in range(3):
                link(v.max(top[:, i, :], lg[:, i, :]))
                link(v.max_index(index8[:, 8 * i:8 * i + 8], top[:, i, :], lg[:, i, :]))
            idx = index8[:, :].rearrange("p (i e) -> p i e", i=3)
            which = R(80, 6, 2)
            link(v.tensor_copy(which, idx[:, :, 0:2]))
            iota8 = bc(iota[:, 0:8], 1, 3)
            v.tensor_tensor(oh1, iota8, which[:, :, 0:1].to_broadcast([128, 3, 8]), ALU.is_equal)
            link(v.tensor_tensor(oh2, iota8, which[:, :, 1:2].to_broadcast([128, 3, 8]), ALU.is_equal))
            v.tensor_tensor(mm_, oh1, oh2, ALU.add).then_inc(picks_counted, 1)
            ex, g1, g2 = R(96, 3, 1), R(100, 3, 1), R(88, 3, 1)
            v.tensor_tensor(ex, top[:, :, 1:2], top[:, :, 0:1], ALU.subtract).then_inc(gates_in, 1)
            dve.wait_ge(gates_exp, 1)
            link(v.tensor_scalar(g1, ex, 1.0, None, ALU.add))
            link(v.reciprocal(g1, g1))
            link(v.tensor_tensor(g2, ex, g1, ALU.mult))
            link(v.tensor_tensor(oh1, oh1, g1.to_broadcast([128, 3, 8]), ALU.mult))
            link(v.tensor_tensor(oh2, oh2, g2.to_broadcast([128, 3, 8]), ALU.mult))
            link(v.tensor_tensor(gate, oh1, oh2, ALU.add))
            dve.wait_ge(count_psum, 1)
            slot0 = R(176)
            v.tensor_copy(slot0[:, 0:2, :], bank[1][:, 32:48].rearrange("p (i e) -> p i e", i=2))
            link(v.tensor_copy(slot0[0:80, 2, :], bank[1][0:80, 48:56]))
            link(v.tensor_tensor(slot0, slot0, mm_, ALU.mult))
            link(v.tensor_scalar(slot0, slot0, -1.0, None, ALU.add))
            per = PASSES * EXPERTS + 1
            slot_of = route[:, 200:200 + 3 * per].rearrange("p (i k) -> p i k", i=3)
            gate_of = route[:, 280:280 + 3 * per].rearrange("p (i k) -> p i k", i=3)
            for b in range(PASSES):
                link(v.tensor_scalar(slot_of[:, :, EXPERTS * b:EXPERTS * b + EXPERTS], slot0, -float(SLOTS * b), None, ALU.add))
                link(v.tensor_copy(gate_of[:, :, EXPERTS * b:EXPERTS * b + EXPERTS], gate))
            link(v.tensor_reduce(route[:, 380:381], bank[1][:, 64:72], AX.X, ALU.max))
            v.tensor_copy(crowded[0:1, 0:1], route[0:1, 380:381]).then_inc(route_ready, 1)
            dve.wait_ge(route_ready, 1)
            for u in range(6):
                i, half = u // 2, u % 2
                n = TILES[i][1]
                dve.wait_ge(comb_psum, u + 1)
                v.tensor_copy(x_tok[0:n, i, 512 * half:512 * half + 512], bank[2 + u][0:n, :]).then_inc(comb_added, 1)

            def picks(k):
                if k is not first_pass:
                    dve.wait_ge(pickT_psum, k)
                for i, (t0, n) in enumerate(TILES):
                    at_slot = slot_of[0:n, i, bass.ds(k, 1)]
                    v.tensor_scalar(pick[0:n, i, :], iota[0:n, 0:SLOTS], at_slot, None, ALU.is_equal)
                    ins = v.tensor_scalar(gpick[0:n, i, :], iota[0:n, 0:SLOTS], at_slot, gate_of[0:n, i, bass.ds(k, 1)], ALU.is_equal, ALU.mult)
                ins.then_inc(pick_ready, 1)

            def expert_pass(k):
                dve.wait_ge(pickT_psum, k + 1)
                dve.wait_ge(comb_psum, 6 * k + 6)
                v.tensor_copy(gpickT, bank[2][0:SLOTS, 0:NT]).then_inc(pickT_ready, 1)
                for c in range(FC):
                    dve.wait_ge(silu_ready, k * FC + (FC + c + 1))
                    v.tensor_tensor(hid[:, c, :], gsil[c % 2], bank[3 + c % 2][:, SLOTS:2 * SLOTS], ALU.mult).then_inc(hid_ready, 1)
                picks(k + 1)
                for u in range(6):
                    i, half = u // 2, u % 2
                    n = TILES[i][1]
                    dve.wait_ge(comb_psum, 6 * k + (u + 7))
                    part = x_tok[0:n, i, 512 * half:512 * half + 512]
                    dve.wait_ge(comb_added, 6 * k + 6)
                    v.tensor_tensor(part, part, bank[5 + u % 3][0:n, :], ALU.add).then_inc(comb_added, 1)

            picks(first_pass)
            with dve.Fori(0, EXPERTS) as e:
                expert_pass(e)
            fullest = dve.value_load(crowded[0:1, 0:1], min_val=0, max_val=NT)
            dve.wait_ge(comb_added, 6 * EXPERTS + 6)
            with dve.If(fullest > SLOTS):
                with dve.Fori(1, PASSES) as b:
                    with dve.Fori(0, EXPERTS) as e:
                        expert_pass(b * EXPERTS + e)
                dve.wait_ge(comb_added, 6 * EXPERTS * PASSES + 6)
            v.memset(route[:, 390:391], 0.0).then_inc(all_added, 1)


def tail_view(raw, k):
    return raw[:, k, NP:RAWC].rearrange("p (j r) -> p j r", r=ST + 3)[:, :, 0:3]


def samples_of_conv(conv, k):
    return conv[:, k, S0:NPAD].rearrange("p (b t) -> p b t", t=ST + 3)[:, :, 0:ST]


_INS = ["x_prompt", "x_sample", "state_ssm", "state_conv", "cache_meta_k", "cache_meta_v", "cache_win_k", "cache_win_v",
        "meta_tokens", "norm_mix_w", "w_in", "conv_w", "conv_b", "dt_bias", "a_log", "d_skip", "ssd_norm_w", "q_norm_w",
        "k_norm_w", "sinks", "attn_norm_w", "w_out", "norm_ffn_w", "w_gate", "w_up", "w_down", "w_router", "moe_w_gate",
        "moe_w_up", "moe_w_down"]
_OUTS = [("y_prompt", (1, 256, 1024)), ("y_sample", (8, 8, 1024)), ("p_ssm", (2, 1, 8, 64, 128)), ("p_conv", (2, 1, 3, 1024)),
         ("p_meta_k", (2, 1, 16, 2, 64)), ("p_meta_v", (2, 1, 16, 2, 64)), ("p_win_k", (2, 1, 128, 2, 64)), ("p_win_v", (2, 1, 128, 2, 64)),
         ("s_ssm", (2, 8, 8, 64, 128)), ("s_conv", (2, 8, 3, 1024)), ("s_win_k", (2, 8, 128, 2, 64)), ("s_win_v", (2, 8, 128, 2, 64))]


def kernel(**inputs):
    import numpy as _np
    import concourse.bacc as _bacc
    from concourse.bass_utils import run_bass_kernel_spmd as _run

    nc = _bacc.Bacc("TRN2", target_bir_lowering=False, num_devices=1)
    arrays, ins, outs = {}, {}, {}
    for name in _INS:
        x = _np.ascontiguousarray(inputs[name])
        arrays[f"in_{name}"] = x
        ins[name] = nc.dram_tensor(f"in_{name}", x.shape, F32, kind="ExternalInput").ap()
    arrays["in_const"] = CONST
    ins["const"] = nc.dram_tensor("in_const", CONST.shape, F32, kind="ExternalInput").ap()
    for name, shape in _OUTS:
        outs[name] = nc.dram_tensor(f"out_{name}", shape, F32, kind="ExternalOutput").ap()
    hymba_step(nc, ins, outs)
    r = _run(nc, [arrays], core_ids=[0])
    return tuple(r.results[0][f"out_{name}"] for name, _ in _OUTS)
```
